# Optimizing a Trainium2 kernel written in Bass

```python
import math
import jax, jax.numpy as jnp
from jax import lax
import numpy as np

D_MODEL = 1024
BATCH = 1
SEQ = 256
DEPTH = 2

CHUNK = 64
Q_BLOCK = 128
EPS = 1e-6
GDN_HEADS = 4
GDN_DK = 128
GDN_DV = 128
GDN_QK_W = GDN_HEADS * GDN_DK
GDN_V_W = GDN_HEADS * GDN_DV
CONV_K = 4
MLA_HEADS = 8
MLA_NOPE = 64
MLA_ROPE = 32
MLA_V = 64
Q_LORA = 384
KV_LORA = 256
ROPE_THETA = 10000.0
N_BRANCH = 2
D_FF = 3584
N_EXPERTS = 8
TOP_K = 2
D_FF_EXPERT = 1792
N_DENSE = (DEPTH + 1) // 2
N_MOE = DEPTH // 2
SPLITS = [GDN_QK_W, GDN_QK_W, GDN_V_W, GDN_V_W, GDN_HEADS, GDN_HEADS,
          Q_LORA, KV_LORA, MLA_ROPE, N_BRANCH * D_MODEL]
IN_COLS = sum(SPLITS)

kernel_name = 'hybrid_gdn_mla_moe_streaming_block'

F32 = jnp.float32

def rmsnorm(x, w):
    xf = x.astype(F32)
    y = xf * lax.rsqrt(jnp.mean(xf * xf, axis=-1, keepdims=True) + EPS)
    return (y * w.astype(F32)).astype(x.dtype)

def l2norm(x):
    return x * lax.rsqrt(jnp.sum(x * x, axis=-1, keepdims=True) + EPS)

def rope(t, cos, sin):
    half = t.shape[-1] // 2
    t1, t2 = t[..., :half].astype(F32), t[..., half:].astype(F32)
    return jnp.concatenate([t1 * cos - t2 * sin, t2 * cos + t1 * sin], axis=-1).astype(t.dtype)

def causal_dwconv(x, w):
    c = x.shape[-1]
    return lax.conv_general_dilated(
        x, w[:, None, :].astype(x.dtype), window_strides=(1,), padding=[(CONV_K - 1, 0)],
        dimension_numbers=('NWC', 'WIO', 'NWC'), feature_group_count=c)

def gated_delta_chunked(q, k, v, g, beta):
    b, s, h, dk = q.shape
    dv = v.shape[-1]
    nc = s // CHUNK

    def chunks(t):
        return t.reshape(b, nc, CHUNK, h, -1).transpose(0, 1, 3, 2, 4)

    qc, kc, vc = chunks(q), chunks(k), chunks(v)
    gc = g.reshape(b, nc, CHUNK, h).transpose(0, 1, 3, 2)
    bc = beta.reshape(b, nc, CHUNK, h).transpose(0, 1, 3, 2)
    G = jnp.cumsum(gc, axis=-1)
    i = jnp.arange(CHUNK)
    incl = i[:, None] >= i[None, :]
    strict = i[:, None] > i[None, :]
    decay = jnp.exp(jnp.where(incl, G[..., :, None] - G[..., None, :], -jnp.inf))
    kb = kc * bc[..., None]
    lower = jnp.where(strict, jnp.einsum('bnhid,bnhjd->bnhij', kb, kc) * decay, 0.0)
    a_mat = lower + jnp.eye(CHUNK, dtype=F32)
    rhs = jnp.concatenate([vc * bc[..., None], kb * jnp.exp(G)[..., None]], axis=-1)
    sol = lax.linalg.triangular_solve(a_mat, rhs, left_side=True, lower=True, unit_diagonal=True)
    u, w = sol[..., :dv], sol[..., dv:]
    intra = jnp.einsum('bnhid,bnhjd->bnhij', qc, kc) * decay
    q_dec = qc * jnp.exp(G)[..., None]
    k_dec = kc * jnp.exp(G[..., -1:] - G)[..., None]
    chunk_decay = jnp.exp(G[..., -1])

    def step(state, inp):
        u_c, w_c, qd, kd, at, cd = inp
        v_new = u_c - jnp.einsum('bhcd,bhde->bhce', w_c, state)
        o = jnp.einsum('bhcd,bhde->bhce', qd, state) + jnp.einsum('bhij,bhje->bhie', at, v_new)
        state = state * cd[..., None, None] + jnp.einsum('bhcd,bhce->bhde', kd, v_new)
        return state, o

    xs = (jnp.moveaxis(u, 1, 0), jnp.moveaxis(w, 1, 0), jnp.moveaxis(q_dec, 1, 0),
          jnp.moveaxis(k_dec, 1, 0), jnp.moveaxis(intra, 1, 0), jnp.moveaxis(chunk_decay, 1, 0))
    s0 = jnp.zeros((b, h, dk, dv), F32)
    _, o = lax.scan(step, s0, xs)
    return o.transpose(1, 0, 3, 2, 4).reshape(b, s, h, dv)

def gdn_branch(q, k, v, z, a, bt, conv_w, a_log, dt_bias, out_norm):
    b, s, _ = q.shape
    qkv = jax.nn.silu(causal_dwconv(jnp.concatenate([q, k, v], axis=-1), conv_w))
    q = qkv[..., :GDN_QK_W].reshape(b, s, GDN_HEADS, GDN_DK).astype(F32)
    k = qkv[..., GDN_QK_W:2 * GDN_QK_W].reshape(b, s, GDN_HEADS, GDN_DK).astype(F32)
    v = qkv[..., 2 * GDN_QK_W:].reshape(b, s, GDN_HEADS, GDN_DV).astype(F32)
    q = l2norm(q) * (GDN_DK ** -0.5)
    k = l2norm(k)
    g = -jnp.exp(a_log.astype(F32)) * jax.nn.softplus(a.astype(F32) + dt_bias.astype(F32))
    beta = jax.nn.sigmoid(bt.astype(F32))
    o = gated_delta_chunked(q, k, v, g, beta)
    o = o * lax.rsqrt(jnp.mean(o * o, axis=-1, keepdims=True) + EPS) * out_norm.astype(F32)
    o = o * jax.nn.silu(z.reshape(b, s, GDN_HEADS, GDN_DV).astype(F32))
    return o.reshape(b, s, GDN_V_W).astype(z.dtype)

def chunk_causal_attention(q, k, v):
    b, s, h, dq = q.shape
    nb = s // Q_BLOCK
    scale = dq ** -0.5
    qb = q.reshape(b, nb, Q_BLOCK, h, dq).transpose(1, 0, 2, 3, 4)
    key_chunk = jnp.arange(s) // CHUNK

    def one_block(args):
        qi, bi = args
        sc = jnp.einsum('bqhd,bkhd->bhqk', qi, k).astype(F32) * scale
        q_chunk = (bi * Q_BLOCK + jnp.arange(Q_BLOCK)) // CHUNK
        mask = key_chunk[None, :] <= q_chunk[:, None]
        p = jax.nn.softmax(jnp.where(mask, sc, -jnp.inf), axis=-1)
        return jnp.einsum('bhqk,bkhe->bqhe', p.astype(v.dtype), v)

    o = lax.map(one_block, (qb, jnp.arange(nb)))
    return o.transpose(1, 0, 2, 3, 4).reshape(b, s, h, v.shape[-1])

def mla_branch(c_q, c_kv, k_r, cos, sin, q_a_norm, w_q_b, kv_a_norm, w_kv_b):
    b, s, _ = c_q.shape
    q = (rmsnorm(c_q, q_a_norm) @ w_q_b).reshape(b, s, MLA_HEADS, MLA_NOPE + MLA_ROPE)
    q_pe = rope(q[..., MLA_NOPE:], cos[:, :, None], sin[:, :, None])
    q = jnp.concatenate([q[..., :MLA_NOPE], q_pe], axis=-1)
    kv = (rmsnorm(c_kv, kv_a_norm) @ w_kv_b).reshape(b, s, MLA_HEADS, MLA_NOPE + MLA_V)
    k_pe = rope(k_r, cos, sin)
    k = jnp.concatenate(
        [kv[..., :MLA_NOPE], jnp.broadcast_to(k_pe[:, :, None, :], (b, s, MLA_HEADS, MLA_ROPE))], axis=-1)
    v = kv[..., MLA_NOPE:]
    o = chunk_causal_attention(q, k, v)
    return o.reshape(b, s, MLA_HEADS * MLA_V)

def swiglu(t, w1, w3, w2):
    return (jax.nn.silu(t @ w1) * (t @ w3)) @ w2

def moe_ffn(h, router_w, w1, w3, w2):
    b, s, d = h.shape
    t = h.reshape(-1, d)
    logits = (t @ router_w).astype(F32)
    top_logits, top_idx = lax.top_k(logits, TOP_K)
    top_w = jax.nn.softmax(top_logits, axis=-1)
    combine = jnp.sum(jax.nn.one_hot(top_idx, N_EXPERTS, dtype=F32) * top_w[..., None], axis=1)
    out = jnp.zeros_like(t)
    for e in range(N_EXPERTS):
        out = out + combine[:, e:e + 1].astype(t.dtype) * swiglu(t, w1[e], w3[e], w2[e])
    return out.reshape(b, s, d)

def setup_inputs(seed: int = 0) -> dict:
    key = jax.random.key(seed)
    ks = jax.random.split(key, 32)
    L = DEPTH

    def nrm(k, shape, fan_in):
        return jax.random.normal(k, shape, F32) * (fan_in ** -0.5)

    def gain(k, shape):
        return 1.0 + 0.02 * jax.random.normal(k, shape, F32)

    x = jax.random.normal(ks[0], (BATCH, SEQ, D_MODEL), F32)
    gaps = jax.random.randint(ks[1], (BATCH, SEQ), 1, 4, dtype=jnp.int32)
    positions = (jnp.cumsum(gaps, axis=1) - gaps[:, :1]).astype(jnp.int32)
    dt = jnp.exp(jax.random.uniform(ks[7], (L, GDN_HEADS), F32, math.log(1e-3), math.log(1e-1)))
    return {
        'x': x,
        'positions': positions,
        'mix_norm': gain(ks[2], (L, D_MODEL)),
        'w_in': nrm(ks[3], (L, D_MODEL, IN_COLS), D_MODEL),
        'gate_bias': 0.01 * jax.random.normal(ks[4], (L, N_BRANCH * D_MODEL), F32),
        'conv_w': nrm(ks[5], (L, CONV_K, 2 * GDN_QK_W + GDN_V_W), CONV_K),
        'a_log': jnp.log(jax.random.uniform(ks[6], (L, GDN_HEADS), F32, 1.0, 16.0)),
        'dt_bias': dt + jnp.log(-jnp.expm1(-dt)),
        'gdn_out_norm': gain(ks[8], (L, GDN_DV)),
        'w_gdn_o': nrm(ks[9], (L, GDN_V_W, D_MODEL), GDN_V_W),
        'q_a_norm': gain(ks[10], (L, Q_LORA)),
        'w_q_b': nrm(ks[11], (L, Q_LORA, MLA_HEADS * (MLA_NOPE + MLA_ROPE)), Q_LORA),
        'kv_a_norm': gain(ks[12], (L, KV_LORA)),
        'w_kv_b': nrm(ks[13], (L, KV_LORA, MLA_HEADS * (MLA_NOPE + MLA_V)), KV_LORA),
        'w_mla_o': nrm(ks[14], (L, MLA_HEADS * MLA_V, D_MODEL), MLA_HEADS * MLA_V),
        'w_out': nrm(ks[15], (L, D_MODEL, D_MODEL), D_MODEL),
        'ffn_norm': gain(ks[16], (L, D_MODEL)),
        'dense_w1': nrm(ks[17], (N_DENSE, D_MODEL, D_FF), D_MODEL),
        'dense_w3': nrm(ks[18], (N_DENSE, D_MODEL, D_FF), D_MODEL),
        'dense_w2': nrm(ks[19], (N_DENSE, D_FF, D_MODEL), D_FF),
        'router_w': nrm(ks[20], (N_MOE, D_MODEL, N_EXPERTS), D_MODEL),
        'moe_w1': nrm(ks[21], (N_MOE, N_EXPERTS, D_MODEL, D_FF_EXPERT), D_MODEL),
        'moe_w3': nrm(ks[22], (N_MOE, N_EXPERTS, D_MODEL, D_FF_EXPERT), D_MODEL),
        'moe_w2': nrm(ks[23], (N_MOE, N_EXPERTS, D_FF_EXPERT, D_MODEL), D_FF_EXPERT),
        'final_norm': gain(ks[24], (D_MODEL,)),
    }

def reference(x, positions, mix_norm, w_in, gate_bias, conv_w, a_log, dt_bias, gdn_out_norm,
              w_gdn_o, q_a_norm, w_q_b, kv_a_norm, w_kv_b, w_mla_o, w_out, ffn_norm,
              dense_w1, dense_w3, dense_w2, router_w, moe_w1, moe_w3, moe_w2, final_norm):
    split_idx = np.cumsum(SPLITS)[:-1].tolist()
    inv_freq = 1.0 / (ROPE_THETA ** (jnp.arange(0, MLA_ROPE, 2, dtype=F32) / MLA_ROPE))
    ang = positions.astype(F32)[..., None] * inv_freq
    cos, sin = jnp.cos(ang), jnp.sin(ang)
    for l in range(DEPTH):
        h = rmsnorm(x, mix_norm[l])
        proj = h @ w_in[l]
        q_g, k_g, v_g, z_g, a_g, b_g, c_q, c_kv, k_r, gate = jnp.split(proj, split_idx, axis=-1)
        o_a = gdn_branch(q_g, k_g, v_g, z_g, a_g, b_g, conv_w[l], a_log[l], dt_bias[l],
                         gdn_out_norm[l]) @ w_gdn_o[l]
        o_b = mla_branch(c_q, c_kv, k_r, cos, sin, q_a_norm[l], w_q_b[l], kv_a_norm[l],
                         w_kv_b[l]) @ w_mla_o[l]
        g = jax.nn.sigmoid((gate + gate_bias[l]).astype(F32)).astype(x.dtype)
        merged = g[..., :D_MODEL] * o_a + g[..., D_MODEL:] * o_b
        x = x + merged @ w_out[l]
        h2 = rmsnorm(x, ffn_norm[l])
        if l % 2 == 0:
            x = x + swiglu(h2, dense_w1[l // 2], dense_w3[l // 2], dense_w2[l // 2])
        else:
            x = x + moe_ffn(h2, router_w[l // 2], moe_w1[l // 2], moe_w3[l // 2], moe_w2[l // 2])
    return rmsnorm(x, final_norm)


_drawn_inputs = setup_inputs


def setup_inputs(seed=0):
    import zlib

    import numpy as np

    out = dict(_drawn_inputs(seed))
    spreads = {}
    factors = {'gate_bias': 5.513,
     'q_a_norm': 4.338,
     'kv_a_norm': 3.185,
     'final_norm': 8.119,
     'gdn_out_norm': 4.205}
    for name, (base, spread) in spreads.items():
        noise = np.random.default_rng([zlib.crc32(name.encode()), seed]).standard_normal(out[name].shape)
        drawn = base * np.exp(spread * noise) if base else spread * noise
        out[name] = __import__('jax').numpy.asarray(drawn.astype(out[name].dtype))
    for name, factor in factors.items():
        out[name] = (out[name] * factor).astype(out[name].dtype)
    return out
```

```python
from contextlib import ExitStack

import numpy as np

import concourse.bass as bass
from concourse import mybir

F32 = mybir.dt.float32
F32R = mybir.dt.float32r
I32 = mybir.dt.int32
U32 = mybir.dt.uint32
ALU = mybir.AluOpType
ACT = mybir.ActivationFunctionType
AX_X = mybir.AxisListType.X

P = 128
RAW = 8
SPL = 4
SLOT = 1024
EPS = 1e-6
BIG = 1e30
CHUNK = 64
TOP_K = 2
ROPE_THETA = 10000.0


class At:

    def __init__(self, c, i=None, per=0):
        self.c, self.i, self.per = c, i, per

    def count(self, k=0):
        return self.c + k if self.i is None else self.i * self.per + (self.c + k)

    def plus(self, k):
        return At(self.c + k, self.i, self.per)

    def landed(self):
        full = 16 * (self.c // RAW + 1)
        return full if self.i is None else self.i * (16 * self.per // RAW) + full


class Chain:

    def __init__(self, eng, sem):
        self.eng, self.sem, self.n, self.i, self.per = eng, sem, 0, None, 0

    def mark(self, ins):
        ins.then_inc(self.sem, 1)
        self.n += 1
        return At(self.n, self.i, self.per).count()

    def wait(self, value):
        self.eng.wait_ge(self.sem, value)

    def link(self, ins):
        self.wait(self.mark(ins))

    def enter(self, i, per):
        self.i, self.per, self.at = i, per, self.n

    def leave(self, times):
        assert self.n - self.at == self.per, (self.n - self.at, self.per)
        self.n = self.at + times * self.per
        self.i = None


def program(nc, A, out):
    _, T, D = A["x"].shape
    L, _, IN = A["w_in"].shape
    TT = T // P
    KC = D // P
    H = A["a_log"].shape[1]
    DV = A["gdn_out_norm"].shape[1]
    QW = H * DV
    NQK = 3 * QW // P
    QL, KVL = A["w_q_b"].shape[1], A["w_kv_b"].shape[1]
    GB = A["gate_bias"].shape[1]
    ROPE = IN - 4 * QW - 2 * H - QL - KVL - GB
    MV = A["w_mla_o"].shape[1]
    QN = A["w_q_b"].shape[2]
    KVN = A["w_kv_b"].shape[2]
    HM = (QN + MV - KVN) // ROPE
    DQ = QN // HM
    NOPE = DQ - ROPE
    VD = MV // HM
    HALF = ROPE // 2
    CONV = A["conv_w"].shape[1]
    FF = A["dense_w1"].shape[2]
    NE, FE = A["moe_w1"].shape[1], A["moe_w1"].shape[3]
    LC = (QL + KVL) // P
    QC = QL // P
    assert T == 256 and D == 1024 and H * P == 512 and DV == P and L == 2 and DQ == 96 and HM == 8
    OFF_Z, OFF_A = 3 * QW, 4 * QW
    OFF_C = OFF_A + 2 * H
    OFF_G = OFF_C + QL + KVL + ROPE
    G1 = OFF_G - OFF_A
    SUB = 448
    HC = FE // 2

    MIX = [("g1", KC), ("z", KC), ("wq", QC), ("wkv", LC - QC), ("qkv", 2 * KC),
           ("gate", 2 * KC), ("gdn_o", QW // P), ("mla_o", MV // P), ("out", KC)]
    first, at = {}, 0
    for name, n in MIX:
        first[name] = at
        at += n
    N_MIX = at
    N_UP = 16
    UPS = FF // (2 * SUB)
    N_DOWN = FF // P
    MIX0, DENSE = 0, N_MIX
    MIX1 = DENSE + UPS * N_UP + N_DOWN
    MOE = MIX1 + N_MIX
    N_EXP = 48
    EC = FE // P
    assert N_UP % RAW == 0 and N_EXP % RAW == 0 and N_UP % SPL == 0 and N_EXP % SPL == 0
    OVER = MOE + NE * N_EXP

    st = ExitStack()
    with st:
        def sb(name, shape, dt=F32, ctx=st):
            return ctx.enter_context(nc.sbuf_tensor(name, shape, dt))

        def sem(name):
            return st.enter_context(nc.semaphore(name))

        raw = sb("raw", [P, RAW, SLOT])
        whi = sb("whi", [P, SPL, SLOT], F32R)
        wlo = sb("wlo", [P, SPL, SLOT], F32R)
        x = sb("x", [P, TT, D])
        hbuf = sb("hbuf", [P, TT, D])
        aT_hi = sb("aT_hi", [P, KC, T], F32R)
        aT_lo = sb("aT_lo", [P, KC, T], F32R)
        rows = sb("rows", [P, 2, D])
        ident = sb("ident", [P, P])
        ident_r = sb("ident_r", [P, P], F32R)
        ones = sb("ones", [P, P])
        incl = sb("incl", [P, P])
        same = sb("same", [P, P])
        upper = sb("upper", [P, P])
        neg_q = sb("neg_q", [P, P])
        neg_k = sb("neg_k", [P, P])
        NLEV = 6
        lev = sb("lev", [P, NLEV, P])
        lev0 = sb("lev0", [P, P])
        slot_no = sb("slot_no", [P, 2, P])
        inchunk = sb("inchunk", [P, 2])
        ids_i = sb("ids_i", [P, P], I32)
        col_i = sb("col_i", [P, 1], I32)
        row_f = sb("row_f", [P, P])
        col_f = sb("col_f", [P, 2])
        epsc = sb("epsc", [P, 1])
        mhalf = sb("mhalf", [P, 16])
        ss = sb("ss", [P, TT])
        rinv = sb("rinv", [P, TT])
        posi = sb("posi", [P, TT], I32)
        ang = sb("ang", [P, 6, TT, HALF])
        cosb = sb("cosb", [P, TT, HALF])
        sinb = sb("sinb", [P, TT, HALF])

        cw_in = sb("cw_in", [CONV * NQK, L, P])
        cw = sb("cw", [P, L, CONV, NQK])
        adt = sb("adt", [P, L, 2, H])
        mix = ExitStack()
        gates = sb("gates", [P, TT, GB], F32, mix)
        pad = gates[:, :, :].rearrange("p a b -> p (a b)")[:, 0:NQK * (T + 4)].rearrange(
            "p (c t) -> p c t", c=NQK)
        PADW = 4
        zs = sb("zs", [P, TT, QW], F32, mix)
        pT_hi = sb("pT_hi", [P, LC, T], F32R, mix)
        pT_lo = sb("pT_lo", [P, LC, T], F32R, mix)
        oT_hi = sb("oT_hi", [P, MV // P, T], F32R, mix)
        oT_lo = sb("oT_lo", [P, MV // P, T], F32R, mix)
        lat_w = sb("lat_w", [P, QL + KVL], F32, mix)
        onorm = sb("onorm", [P, DV], F32, mix)
        abr = sb("abr", [P, TT, 2 * H], F32, mix)
        sp = sb("sp", [P, 6, TT, H], F32, mix)
        gl = sb("gl", [P, TT, H], F32, mix)
        beta = sb("beta", [P, TT, H], F32, mix)
        krr = sb("krr", [P, TT, ROPE], F32, mix)
        lss = sb("lss", [P, TT, 2], F32, mix)
        lri = sb("lri", [P, TT, 2], F32, mix)
        tmp_r = sb("tmp_r", [P, 2, HM, HALF], F32, mix)
        mx = sb("mx", [P, 3, HM], F32, mix)
        rs = sb("rs", [P, 3, HM], F32, mix)
        ri = sb("ri", [P, 3, HM], F32, mix)
        sums = sb("sums", [P, 64], F32, mix)
        gcol = sb("gcol", [P, 10, TT, H], F32, mix)
        cdb = sb("cdb", [P, 4, H], F32, mix)
        oss = sb("oss", [P, TT, H], F32, mix)
        ori = sb("ori", [P, TT, H], F32, mix)
        mla = ExitStack()
        qT = sb("qT", [DQ, HM, T], F32, mla)
        kT = sb("kT", [DQ, HM, T], F32, mla)
        vm = sb("vm", [P, TT, MV], F32, mla)
        om = sb("om", [P, TT, MV], F32, mla)
        stage1 = ExitStack()
        lat = sb("lat", [P, TT, QL + KVL], F32, stage1)
        qm = sb("qm", [P, TT, HM, DQ], F32, stage1)
        km = sb("km", [P, TT, HM, DQ], F32, stage1)
        stage1.close()
        stage2 = ExitStack()
        prob = sb("prob", [P, 2, D], F32, stage2)
        probT = sb("probT", [P, 2, D], F32, stage2)
        stage2.close()
        mla.close()
        gdn = ExitStack()
        qkv = sb("qkv", [P, NQK, T], F32, gdn)
        wTb = qkv[:, 0:4, :]
        ub = qkv[:, 4:8, :].rearrange("p a b -> p (a b)").rearrange("p (t n) -> p t n", t=TT)
        vnb = qkv[:, 8:12, :].rearrange("p a b -> p (a b)").rearrange("p (t n) -> p t n", t=TT)
        kb = sb("kb", [P, TT, QW], F32, gdn)
        kd = sb("kd", [P, TT, QW], F32, gdn)
        vb = sb("vb", [P, TT, QW], F32, gdn)
        Lm = sb("Lm", [P, TT, QW], F32, gdn)
        LT = sb("LT", [P, TT, QW], F32, gdn)
        X = sb("X", [P, TT, QW], F32, gdn)
        XT = sb("XT", [P, TT, QW], F32, gdn)
        MT = sb("MT", [P, TT, QW], F32, gdn)
        S = sb("S", [P, 2, QW], F32, gdn)
        gdn.close()
        mix.close()
        hflat = hbuf[:, :, :].rearrange("p a b -> p (a b)")
        inT = hflat[:, 0:TT * QW].rearrange("p (t n) -> p t n", t=TT)
        qdT = hflat[:, TT * QW:2 * TT * QW].rearrange("p (h t) -> p h t", h=H)

        dns = ExitStack()
        dT_hi = sb("dT_hi", [P, N_DOWN, T], F32R, dns)
        dT_lo = sb("dT_lo", [P, N_DOWN, T], F32R, dns)
        dhid = sb("dhid", [P, TT, 2 * SUB], F32, dns)
        dsil = sb("dsil", [P, 2, TT, SUB], F32, dns)
        dns.close()
        moe = ExitStack()
        h2_hi = sb("h2_hi", [P, TT, D], F32R, moe)
        h2_lo = sb("h2_lo", [P, TT, D], F32R, moe)
        h2T = sb("h2T", [P, KC, T], F32, moe)
        rw = sb("rw", [P, KC, NE], F32, moe)
        gT_hi = sb("gT_hi", [P, KC, P], F32R, moe)
        gT_lo = sb("gT_lo", [P, KC, P], F32R, moe)
        ehid = sb("ehid", [P, FE], F32, moe)
        esil = sb("esil", [P, HC], F32, moe)
        eT_hi = sb("eT_hi", [P, EC, P], F32R, moe)
        eT_lo = sb("eT_lo", [P, EC, P], F32R, moe)
        y_hi = sb("y_hi", [P, D], F32R, moe)
        y_lo = sb("y_lo", [P, D], F32R, moe)
        sel = sb("sel", [P, TT, P], F32R, moe)
        selT = sb("selT", [P, T], F32R, moe)
        lg = sb("lg", [P, TT, NE], F32, moe)
        top = sb("top", [P, TT, 8], F32, moe)
        topi = sb("topi", [P, TT, 8], U32, moe)
        topf = sb("topf", [P, TT, 2], F32, moe)
        tw = sb("tw", [P, TT, 4], F32, moe)
        oneh = sb("oneh", [P, 2, TT, NE], F32, moe)
        mask = sb("mask", [P, TT, NE], F32, moe)
        comb = sb("comb", [P, TT, NE + 1], F32, moe)
        rank = sb("rank", [P, TT, NE + 1], F32, moe)
        cmax = sb("cmax", [P, 2], F32, moe)
        flag = sb("flag", [P, 1], I32, moe)
        moe.close()

        ps = st.enter_context(nc.psum_tensor("ps", [P, 8, 512], F32))

        def two(b):
            return ps[:, b:b + 2, :].rearrange("p a b -> p (a b)")

        s_raw = [sem(f"s_raw{i}") for i in range(RAW)]
        w_hi = sem("w_hi")
        w_lo = sem("w_lo")
        w_used = sem("w_used")
        s_x = sem("s_x")
        s_small = [sem(f"s_small{i}") for i in range(8)]
        s_row = [sem("s_row0"), sem("s_row1")]
        row_used = sem("row_used")
        s_out = sem("s_out")
        chain_v, chain_a, chain_p = sem("chain_v"), sem("chain_a"), sem("chain_p")
        names = """ids consts norm_ss norm_r norm_h norm_T norm_hi norm_lo cwT cw_ready
            z_ready lat_ss lat_r lat_h lat_T lat_hi lat_lo g1_used g_ready
            q_copied q_rope kv_copied k_rope qk_T qk_Tc sc_done sc_masked sc_exp
            p_T p_Tc pv_done o_norm om_T om_hi om_lo pad_ready tap0 conv_done qkv_ready
            sq_ready sums_done sums_used lnrow lncols cols_ready row_done row_exp
            eq_in e_exp kk_done L_ready LT_done LT_ready kt_done kt_used inv_ready
            y_done y_ready zz_done x_ready w_done w_ready u_ready v_done vn_ready o_done s_done
            s_ready o_ss o_r og_ready og_T og_hi og_lo gate_in gate_ready
            oa_in merged m_T m_hi m_lo x_new
            h1_used h3_used hT_done hT_hi hT_lo
            sel_in lg_done lg_ready e_ready rank_done rank_ready sel_ready selT_done
            selT_used gat_done gat_hi
            ey_hi ey_lo sct_done sct_used over_done trig""".split()
        s = {n: sem(n) for n in names}

        block = st.enter_context(nc.Block())

        def src2(w, rows0, c0, c1):
            return w[rows0:rows0 + P, c0:c1]

        def mix_tiles(l):
            w = A["w_in"][l]
            o = [src2(w, k * P, OFF_A, OFF_G) for k in range(KC)]
            o += [src2(w, k * P, OFF_Z, OFF_A) for k in range(KC)]
            o += [src2(A["w_q_b"][l], k * P, 0, QN) for k in range(QC)]
            o += [src2(A["w_kv_b"][l], k * P, 0, KVN) for k in range(LC - QC)]
            for hf in range(2):
                o += [src2(w, k * P, hf * 3 * QW // 2, (hf + 1) * 3 * QW // 2) for k in range(KC)]
            for hf in range(2):
                o += [src2(w, k * P, OFF_G + hf * D, OFF_G + (hf + 1) * D) for k in range(KC)]
            o += [src2(A["w_gdn_o"][l], k * P, 0, D) for k in range(QW // P)]
            o += [src2(A["w_mla_o"][l], k * P, 0, D) for k in range(MV // P)]
            o += [src2(A["w_out"][l], k * P, 0, D) for k in range(KC)]
            return o

        MIX_COLS = [v.shape[1] for v in mix_tiles(0)]
        EXP_COLS = [HC] * (4 * KC) + [D] * (EC - 2) + [D // 2] * 4

        @block.sync
        def _(sync):
            def load(t, dst, src):
                if t.c >= RAW:
                    sync.wait_ge(w_lo, t.count(1 - RAW))
                sync.dma_start(dst, src).then_inc(s_raw[t.c % RAW], 16)

            def slot(t, n):
                return raw[:, t.c % RAW, 0:n]

            def mixer(l, base):
                for j, src in enumerate(mix_tiles(l)):
                    t = At(base + j)
                    load(t, slot(t, src.shape[1]), src)

            sync.dma_start(x[:, :, :], A["x"][0].rearrange("(t p) d -> p t d", p=P)).then_inc(s_x, 16)
            mixer(0, MIX0)
            with sync.Fori(0, UPS) as i:
                for sub in range(2):
                    for wi, w in enumerate((A["dense_w1"][0], A["dense_w3"][0])):
                        for k in range(4):
                            t = At(DENSE + sub * 8 + wi * 4 + k, i, N_UP)
                            src = w[2 * P * k:2 * P * (k + 1), bass.ds(i * (2 * SUB) + sub * SUB, SUB)]
                            load(t, slot(t, 2 * SUB).rearrange("p (a n) -> p a n", a=2),
                                 src.rearrange("(a p) n -> p a n", p=P))
            for k in range(N_DOWN):
                t = At(DENSE + UPS * N_UP + k)
                load(t, slot(t, D), src2(A["dense_w2"][0], k * P, 0, D))
            mixer(1, MIX1)

            def experts(base):
                w1 = A["moe_w1"][0].rearrange("e d f -> (e d) f")
                w3 = A["moe_w3"][0].rearrange("e d f -> (e d) f")
                w2 = A["moe_w2"][0].rearrange("e f d -> (e f) d")
                with sync.Fori(0, NE) as e:
                    j = 0
                    for hf in range(2):
                        for w in (w1, w3):
                            for k in range(KC):
                                t = At(base + j, e, N_EXP)
                                load(t, slot(t, HC), w[bass.ds(e * D + k * P, P), hf * HC:(hf + 1) * HC])
                                j += 1
                    for k in range(EC):
                        for c in ([0] if k < EC - 2 else [0, 1]):
                            n = EXP_COLS[j]
                            t = At(base + j, e, N_EXP)
                            load(t, slot(t, n), w2[bass.ds(e * FE + k * P, P), c * n:(c + 1) * n])
                            j += 1
                    assert j == N_EXP

            experts(MOE)
            sync.wait_ge(s["rank_ready"], 2)
            over = sync.value_load(flag[0:1, 0:1], min_val=0, max_val=1)
            with sync.If(over):
                experts(OVER)
            sync.wait_ge(s["norm_h"], 2 * 5)
            sync.dma_start(out[0].rearrange("(t p) d -> p t d", p=P), hbuf[:, :, :]).then_inc(s_out, 16)
            sync.wait_ge(s_out, 16)

        @block.gpsimd
        def _(pool):
            ch = Chain(pool, chain_p)
            pool.iota(ids_i[:, :], pattern=[[1, P]], base=0, channel_multiplier=0).then_inc(s["ids"], 1)
            pool.iota(col_i[:, :], pattern=[[0, 1]], base=0, channel_multiplier=1).then_inc(s["ids"], 1)
            pool.memset(mhalf[:, :], -0.5).then_inc(s["ids"], 1)
            pool.memset(ones[:, :], 1.0).then_inc(s["ids"], 1)
            pool.memset(epsc[:, :], EPS).then_inc(s["ids"], 1)
            pool.wait_ge(s["ids"], 5)
            seq = []
            for l in range(L):
                seq += [A["mix_norm"][l], A["gate_bias"][l, 0:D], A["gate_bias"][l, D:2 * D], A["ffn_norm"][l]]
            seq.append(A["final_norm"][:])

            def row(r):
                if r >= 2:
                    pool.wait_ge(row_used, r - 1)
                pool.dma_start(rows[:, r % 2, :], seq[r].rearrange("(a d) -> a d", a=1).to_broadcast([P, D])
                               ).then_inc(s_row[r % 2], 16)

            def small(i, dst, src):
                pool.dma_start(dst, src).then_inc(s_small[i], 16)

            def bc(v, n):
                return v.rearrange("(a d) -> a d", a=1).to_broadcast([P, n])

            row(0)
            with nc.allow_non_contiguous_dma(reason="256 positions"):
                small(0, posi[:, :], A["positions"][0].rearrange("(t p) -> p t", p=P))
            small(1, cw_in[:, :, :], A["conv_w"].rearrange("l k (c p) -> (k c) l p", p=P) if False else
                  A["conv_w"].rearrange("l k (c p) -> l (k c) p", p=P).rearrange("l a p -> a l p"))
            small(2, adt[:, :, 0, :], A["a_log"].rearrange("(o l) h -> o l h", o=1).to_broadcast([P, L, H]))
            small(3, adt[:, :, 1, :], A["dt_bias"].rearrange("(o l) h -> o l h", o=1).to_broadcast([P, L, H]))

            def rms_scale(dst, src, n):
                w = src.shape[-1] if len(src.shape) == 2 else src.shape[-1] * src.shape[-2]
                ch.link(pool.tensor_scalar(dst, src, 1.0 / n, EPS, ALU.mult, ALU.add))
                return pool.tensor_tensor(dst, dst, mhalf[:, 0:w] if len(src.shape) == 2 else
                                          mhalf[:, 0:w].rearrange("p (a b) -> p a b", a=src.shape[-2]), ALU.pow)

            def norm(n):
                pool.wait_ge(s["norm_ss"], TT * (n + 1))
                rms_scale(rinv[:, :], ss[:, :], D).then_inc(s["norm_r"], 1)

            for l in range(L):
                small(4, lat_w[:, 0:QL], bc(A["q_a_norm"][l], QL))
                small(5, lat_w[:, QL:QL + KVL], bc(A["kv_a_norm"][l], KVL))
                small(6, onorm[:, :], bc(A["gdn_out_norm"][l], DV))
                norm(2 * l)
                row(4 * l + 1)
                pool.wait_ge(s["lat_ss"], 4 * (l + 1))
                for j, n in enumerate((QL, KVL)):
                    rms_scale(lri[:, :, j], lss[:, :, j], n).then_inc(s["lat_r"], 1)
                row(4 * l + 2)
                pool.wait_ge(s["o_ss"], TT * (l + 1))
                rms_scale(ori[:, :, :], oss[:, :, :], DV).then_inc(s["o_r"], 1)
                row(4 * l + 3)
                norm(2 * l + 1)
                row(4 * l + 4)
                if l == 0:
                    pool.wait_ge(s["x_new"], 2 * TT)
            with nc.allow_non_contiguous_dma(reason="rows of 8 router weights"):
                small(7, rw[:, :, :], A["router_w"][0].rearrange("(k p) e -> p k e", p=P))
            pool.wait_ge(s["rank_ready"], 2)
            norm(2 * L)
            pool.wait_ge(s_small[7], 16)

        @block.scalar
        def _(act):
            ch = Chain(act, chain_a)
            a = nc.scalar.activation
            done = [0]

            def split(t, n):
                act.wait_ge(s_raw[t.c % RAW], t.landed())
                if t.c >= SPL:
                    act.wait_ge(w_used, t.count(1 - SPL))
                a(whi[:, t.c % SPL, 0:n], raw[:, t.c % RAW, 0:n], ACT.Copy).then_inc(w_hi, 1)

            def upto(base, n):
                while done[0] < min(base + n, base + N_MIX):
                    split(At(done[0]), MIX_COLS[done[0] - base])
                    done[0] += 1

            def norm(n, split_T=True):
                for t in range(TT):
                    a(hbuf[:, t, :], x[:, t, :], ACT.Square, accum_out=ss[:, t:t + 1]).then_inc(s["norm_ss"], 1)
                if n == 2 * L:
                    return
                for t in range(TT):
                    act.wait_ge(s["norm_T"], TT * n + t + 1)
                    src = two(4 + 2 * t).rearrange("p (k n) -> p k n", k=KC)
                    if split_T:
                        a(aT_hi[:, :, t * P:(t + 1) * P], src, ACT.Copy).then_inc(s["norm_hi"], 1)
                    else:
                        a(h2T[:, :, t * P:(t + 1) * P], src, ACT.Copy).then_inc(s["norm_hi"], 1)

            act.wait_ge(s["trig"], 1)
            a(sinb[:, :, :], ang[:, 0, :, :], ACT.Sin).then_inc(s["trig"], 1)
            a(cosb[:, :, :], ang[:, 1, :, :], ACT.Sin).then_inc(s["trig"], 1)
            act.wait_ge(s["cwT"], L)
            for l in range(L):
                a(cw[:, l, :, :], ps[:, l, 0:CONV * NQK].rearrange("p (k c) -> p k c", k=CONV),
                  ACT.Copy).then_inc(s["cw_ready"], 1)
            act.wait_ge(s_x, 16)

            for l in range(L):
                base = (MIX0, MIX1)[l]
                done[0] = base
                norm(2 * l)
                upto(base, first["z"] + SPL - 1)
                act.wait_ge(w_used, base + first["z"])
                for t in range(TT):
                    v = two(2 * t)[:, 0:G1]
                    a(abr[:, t, :], v[:, 0:2 * H], ACT.Copy).then_inc(s["g1_used"], 1)
                    a(krr[:, t, :], v[:, G1 - ROPE:G1], ACT.Copy).then_inc(s["g1_used"], 1)
                    a(lat[:, t, :], v[:, 2 * H:2 * H + QL + KVL], ACT.Copy).then_inc(s["g1_used"], 1)
                act.wait_ge(s["g1_used"], 6 * (l + 1))
                for t in range(TT):
                    a(om[:, t, 0:QL], lat[:, t, 0:QL], ACT.Square,
                      accum_out=lss[:, t, 0:1]).then_inc(s["lat_ss"], 1)
                    a(vm[:, t, 0:KVL], lat[:, t, QL:QL + KVL], ACT.Square,
                      accum_out=lss[:, t, 1:2]).then_inc(s["lat_ss"], 1)
                upto(base, first["z"] + 6)
                act.wait_ge(s["g_ready"], 3 * l + 1)
                ch.link(a(sp[:, 2, :, :], sp[:, 1, :, :], ACT.Exp))
                ch.link(a(sp[:, 3, :, :], sp[:, 2, :, :], ACT.Ln, bias=1.0))
                ch.link(a(sp[:, 4, :, :], abr[:, :, H:2 * H], ACT.Exp, scale=-1.0))
                a(adt[:, l, 0, :], adt[:, l, 0, :], ACT.Exp).then_inc(s["g_ready"], 1)
                upto(base, first["wq"] + SPL - 1)
                act.wait_ge(w_used, base + first["wq"])
                for t in range(TT):
                    a(zs[:, t, :], ps[:, 4 + t, :], ACT.Silu).then_inc(s["z_ready"], 1)
                for t in range(TT):
                    act.wait_ge(s["lat_T"], TT * l + t + 1)
                    a(pT_hi[:, :, t * P:(t + 1) * P], two(6)[:, 0:LC * P].rearrange("p (k n) -> p k n", k=LC),
                      ACT.Copy).then_inc(s["lat_hi"], 1)
                upto(base, first["qkv"] + 2)
                act.wait_ge(w_used, base + first["wkv"])
                for t in range(TT):
                    a(qm[:, t, :, :], two(4 + 2 * t)[:, 0:QN].rearrange("p (h d) -> p h d", h=HM),
                      ACT.Copy).then_inc(s["q_copied"], 1)
                act.wait_ge(w_used, base + first["qkv"])
                for t in range(TT):
                    v = two(2 * t)[:, 0:KVN].rearrange("p (h d) -> p h d", h=HM)
                    a(km[:, t, :, 0:NOPE], v[:, :, 0:NOPE], ACT.Copy).then_inc(s["kv_copied"], 1)
                    a(vm[:, t, :].rearrange("p (h d) -> p h d", h=HM), v[:, :, NOPE:NOPE + VD],
                      ACT.Copy).then_inc(s["kv_copied"], 1)
                for u in range(4):
                    upto(base, first["qkv"] + 4 + 2 * (u // 2) + 2)
                    act.wait_ge(s["qk_T"], 4 * l + u + 1)
                    dst = (qT, kT)[u // 2]
                    a(dst[:, :, (u % 2) * P:(u % 2 + 1) * P],
                      two(4 + 2 * (u % 2))[0:DQ, :].rearrange("p (h n) -> p h n", h=HM),
                      ACT.Copy).then_inc(s["qk_Tc"], 1)

                def evac_qkv(hf):
                    act.wait_ge(w_used, base + first["qkv"] + KC * (hf + 1))
                    n = NQK // 2
                    a(pad[:, hf * n:(hf + 1) * n, 3:3 + T],
                      ps[:, 0:3, :].rearrange("p a (b t) -> p (a b) t", b=2), ACT.Copy).then_inc(s["pad_ready"], 1)

                def exps(u):
                    nh, nk = (HM, P) if u == 0 else (HM // 2, T)
                    act.wait_ge(s["sc_masked"], 3 * l + u + 1)
                    if u == 2:
                        act.wait_ge(s["p_T"], 3 * l + 1)
                    for h in range(nh):
                        a(prob[:, u % 2, h * nk:(h + 1) * nk], two(3)[:, h * nk:(h + 1) * nk], ACT.Exp,
                          bias=mx[:, u, h:h + 1], scale=float(DQ) ** -0.5,
                          accum_out=rs[:, u, h:h + 1]).then_inc(s["sc_exp"], 1)

                def probs_T(u):
                    act.wait_ge(s["p_T"], 3 * l + u + 1)
                    if u == 2:
                        act.wait_ge(s["pv_done"], 3 * l + 1)
                    a(probT[:, u % 2, :], two(5), ACT.Copy).then_inc(s["p_Tc"], 1)

                upto(base, first["qkv"] + 10)
                evac_qkv(0)
                exps(0)
                upto(base, first["qkv"] + 12)
                probs_T(0)
                exps(1)
                upto(base, first["qkv"] + 14)
                probs_T(1)
                exps(2)
                upto(base, first["qkv"] + 16)
                probs_T(2)
                evac_qkv(1)
                upto(base, first["gate"] + 3)
                for t in range(TT):
                    act.wait_ge(s["om_T"], TT * l + t + 1)
                    a(oT_hi[:, :, t * P:(t + 1) * P], ps[:, 4 + t, :].rearrange("p (k n) -> p k n", n=P),
                      ACT.Copy).then_inc(s["om_hi"], 1)
                act.wait_ge(s["pad_ready"], 3 * l + 3)
                act.wait_ge(s["om_T"], TT * (l + 1))
                act.wait_ge(s["o_norm"], 2 * (l + 1))
                for c in range(NQK):
                    a(qkv[:, c, :], pad[:, c, 0:T], ACT.Copy, scale=cw[:, l, 0, c:c + 1]).then_inc(s["tap0"], 1)
                upto(base, first["gate"] + 4)
                act.wait_ge(s["conv_done"], l + 1)
                for hf in range(3):
                    v = qkv[:, hf * H:(hf + 1) * H, :]
                    a(v, v, ACT.Silu).then_inc(s["qkv_ready"], 1)
                act.wait_ge(s["qkv_ready"], 3 * (l + 1))
                sq = X[:, :, :].rearrange("p a b -> p (a b)"), XT[:, :, :].rearrange("p a b -> p (a b)")
                for j in range(2):
                    a(sq[j].rearrange("p (c t) -> p c t", c=H), qkv[:, j * H:(j + 1) * H, :],
                      ACT.Square).then_inc(s["sq_ready"], 1)
                upto(base, first["gate"] + 7)
                act.wait_ge(s["sums_used"], l + 1)
                a(gcol[:, 0:2, :, :], sums[:, 0:16].rearrange("p (j t h) -> p j t h", j=2, t=TT), ACT.Ln,
                  bias=epsc[:, 0:1]).then_inc(s["lnrow"], 1)
                act.wait_ge(s["lncols"], l + 1)
                ch.link(a(gcol[:, 7, :, :], gcol[:, 4, :, :], ACT.Exp))
                ch.link(a(cdb[:, :, :], sums[:, 32:48].rearrange("p (c h) -> p c h", c=4), ACT.Exp))
                a(gcol[:, 8, :, :], gcol[:, 6, :, :], ACT.Exp).then_inc(s["cols_ready"], 1)
                upto(base, first["gate"] + 8)
                for t in range(TT):
                    act.wait_ge(s["row_done"], TT * l + t + 1)
                    a(qdT[:, :, t * P:(t + 1) * P], ps[:, 4 + t, :].rearrange("p (h n) -> p h n", h=H),
                      ACT.Exp).then_inc(s["row_exp"], 1)
                for t in range(TT):
                    act.wait_ge(s["eq_in"], TT * l + t + 1)
                    for h in range(H):
                        hs = slice(h * P, (h + 1) * P)
                        a(inT[:, t, hs], inT[:, t, hs], ACT.Exp, bias=gcol[:, 5, t, h:h + 1]).then_inc(s["e_exp"], 1)
                        a(Lm[:, t, hs], Lm[:, t, hs], ACT.Exp, scale=-1.0,
                          bias=gcol[:, 4, t, h:h + 1]).then_inc(s["e_exp"], 1)
                upto(base, first["gate"] + 9)
                for t in range(TT):
                    act.wait_ge(s["LT_done"], TT * l + t + 1)
                    a(LT[:, t, :], ps[:, 4 + t, :], ACT.Copy).then_inc(s["LT_ready"], 1)
                for k in range(1, NLEV):
                    upto(base, first["gate"] + 10 + k)
                    for t in range(TT):
                        act.wait_ge(s["y_done"], (5 * l + k - 1) * TT + t + 1)
                        a(Lm[:, t, :], ps[:, 4 + t, :], ACT.Copy).then_inc(s["y_ready"], 1)
                    if k == 1:
                        act.wait_ge(s["gate_in"], 4 * l + 2)
                        for t in range(TT):
                            v = gates[:, t, 0:D]
                            a(v, v, ACT.Sigmoid).then_inc(s["gate_ready"], 1)
                upto(base, first["gate"] + 16)
                for t in range(TT):
                    act.wait_ge(s["w_done"], TT * l + t + 1)
                    a(wTb[:, :, t * P:(t + 1) * P], ps[:, 4 + t, :].rearrange("p (h n) -> p h n", h=H),
                      ACT.Copy).then_inc(s["w_ready"], 1)
                upto(base, first["gdn_o"] + 3)
                for t in range(TT):
                    act.wait_ge(s["og_T"], TT * l + t + 1)
                    a(pT_hi[:, 0:H, t * P:(t + 1) * P], ps[:, 4 + t, :].rearrange("p (k n) -> p k n", n=P),
                      ACT.Copy).then_inc(s["og_hi"], 1)
                act.wait_ge(s["gate_in"], 4 * (l + 1))
                for t in range(TT):
                    v = gates[:, t, D:2 * D]
                    a(v, v, ACT.Sigmoid).then_inc(s["gate_ready"], 1)
                upto(base, first["out"] + 2)
                for t in range(TT):
                    act.wait_ge(s["m_T"], TT * l + t + 1)
                    a(aT_hi[:, :, t * P:(t + 1) * P], two(2 * t).rearrange("p (k n) -> p k n", k=KC),
                      ACT.Copy).then_inc(s["m_hi"], 1)
                upto(base, N_MIX)
                act.wait_ge(s["x_new"], (TT * 2) * l + TT)
                if l == 0:
                    norm(1)

                    def transposed(i, d):
                        for t in range(TT):
                            act.wait_ge(s["hT_done"], At(t + 1 - d * TT, i, TT).count())
                            k0 = 0 if i is None else i * 7 - 7 * d
                            a(dT_hi[:, bass.ds(k0, 7), t * P:(t + 1) * P],
                              two(4 + 2 * t)[:, 0:2 * SUB].rearrange("p (k n) -> p k n", n=P),
                              ACT.Copy).then_inc(s["hT_hi"], 1)

                    def up(i):
                        for j in range(N_UP):
                            split(At(DENSE + j, i, N_UP), 2 * SUB)
                            if j == 3 + SPL and i is not None:
                                transposed(i, 1)
                            if j in (7, 15):
                                act.wait_ge(w_used, At(DENSE + j - 3, i, N_UP).count())
                                sub = j // 8
                                a(dsil[:, sub, :, :], ps[:, 0:TT, 0:SUB], ACT.Silu).then_inc(s["h1_used"], 1)

                    up(None)
                    with act.Fori(1, UPS) as i:
                        up(i)
                    split(At(MIX1 - N_DOWN), D)
                    for t in range(TT):
                        act.wait_ge(s["hT_done"], TT * (UPS - 1) + t + 1)
                        a(dT_hi[:, N_DOWN - 7:N_DOWN, t * P:(t + 1) * P],
                          two(4 + 2 * t)[:, 0:2 * SUB].rearrange("p (k n) -> p k n", n=P),
                          ACT.Copy).then_inc(s["hT_hi"], 1)
                    for k in range(1, N_DOWN):
                        split(At(DENSE + UPS * N_UP + k), D)
                    act.wait_ge(s["x_new"], 2 * TT)
                else:
                    norm(3, False)
                    for t in range(TT):
                        act.wait_ge(s["sel_in"], t + 1)
                        a(h2_hi[:, t, :], hbuf[:, t, :], ACT.Copy).then_inc(s["e_ready"], 1)
                    act.wait_ge(s["lg_ready"], 1)
                    a(tw[:, :, 1:2], tw[:, :, 0:1], ACT.Exp).then_inc(s["e_ready"], 1)

                    def gathered(e, c, k):
                        act.wait_ge(s["gat_done"], At(c + k + 1, e, 2).count())
                        dst = (gT_hi, gT_lo)[k]
                        a(dst[:, :, :], two(6).rearrange("p (k n) -> p k n", k=KC), ACT.Copy).then_inc(s["gat_hi"], 1)

                    def experts(base, r):
                        for k in range(2):
                            gathered(None, 18 * r, k)
                        with act.Fori(0, NE) as e:
                            def halves(c):
                                return At(8 + 16 * r + c, e, 2).count()

                            for j in range(N_EXP):
                                split(At(base + j, e, N_EXP), EXP_COLS[j])
                                if j in (3 + 8, 3 + 24):
                                    hf = j // 16
                                    act.wait_ge(w_used, At(base + (2 * hf + 1) * KC, e, N_EXP).count())
                                    act.wait_ge(s["h3_used"], halves(hf))
                                    a(esil[:, :].rearrange("p (a n) -> p a n", a=2), ps[:, 0:2, 0:HC // 2],
                                      ACT.Silu).then_inc(s["h1_used"], 1)
                                if j == 15:
                                    act.wait_ge(s["selT_done"], At(8 * r + 1, e, 1).count())
                                    a(selT[:, :], ps[:, 6, 0:T], ACT.Copy).then_inc(s["selT_used"], 1)
                                if j in (22, 38):
                                    hf = j // 32
                                    cs = slice(hf * EC // 2, (hf + 1) * EC // 2)
                                    act.wait_ge(s["hT_done"], halves(hf + 1))
                                    a(eT_hi[:, cs, :], two(6)[:, 0:HC].rearrange("p (k n) -> p k n", n=P),
                                      ACT.Copy).then_inc(s["hT_hi"], 1)
                                if j == 35:
                                    gathered(e, 18 * r + 2, 0)
                                if j == 45:
                                    gathered(e, 18 * r + 2, 1)
                            act.wait_ge(w_used, At(base + N_EXP, e, N_EXP).count())
                            a(y_hi[:, :], two(4), ACT.Copy).then_inc(s["ey_hi"], 1)

                    experts(MOE, 0)
                    act.wait_ge(s["rank_ready"], 2)
                    over = act.value_load(flag[0:1, 0:1], min_val=0, max_val=1)
                    with act.If(over):
                        experts(OVER, 1)
                    act.wait_ge(s["over_done"], 1)
                    norm(2 * L)

        @block.vector
        def _(dve):
            v = nc.vector
            ch = Chain(dve, chain_v)
            link, mark = ch.link, ch.mark
            done = [0]
            tt, ts, stt = v.tensor_tensor, v.tensor_scalar, v.scalar_tensor_tensor

            def split(t, n):
                dve.wait_ge(w_hi, t.count(1))
                tt(wlo[:, t.c % SPL, 0:n], raw[:, t.c % RAW, 0:n], whi[:, t.c % SPL, 0:n].bitcast(F32),
                   ALU.subtract).then_inc(w_lo, 1)

            def upto(base, n):
                while done[0] < min(base + n, base + N_MIX):
                    split(At(done[0]), MIX_COLS[done[0] - base])
                    done[0] += 1

            dve.wait_ge(s["ids"], 5)
            link(v.tensor_copy(row_f[:, :], ids_i[:, :]))
            link(v.tensor_copy(col_f[:, 0:1], col_i[:, :]))
            for r in range(2):
                link(ts(slot_no[:, r, :], row_f[:, :], float(1 + r * P), None, ALU.add))
            link(ts(ident[:, :], row_f[:, :], col_f[:, 0:1], None, ALU.is_equal))
            link(v.tensor_copy(ident_r[:, :], ident[:, :]))
            link(ts(upper[:, :], row_f[:, :], col_f[:, 0:1], None, ALU.is_gt))
            link(ts(neg_q[:, :], row_f[:, :], col_f[:, 0:1], None, ALU.is_lt))
            link(v.tensor_copy(same[:, :], ident[:, :]))
            for k in range(NLEV):
                link(ts(ids_i[:, :], ids_i[:, :], 1, None, ALU.arith_shift_right))
                link(ts(col_i[:, :], col_i[:, :], 1, None, ALU.arith_shift_right))
                link(v.tensor_copy(row_f[:, :], ids_i[:, :]))
                link(v.tensor_copy(col_f[:, 1:2], col_i[:, :]))
                link(ts(row_f[:, :], row_f[:, :], col_f[:, 1:2], None, ALU.is_equal))
                link(tt(lev[:, k, :], row_f[:, :], same[:, :], ALU.subtract))
                link(v.tensor_copy(same[:, :], row_f[:, :]))
            link(tt(lev0[:, :], lev[:, 0, :], neg_q[:, :], ALU.mult))
            for k in range(NLEV):
                link(tt(lev[:, k, :], lev[:, k, :], upper[:, :], ALU.mult))
            link(ts(inchunk[:, 1:2], col_f[:, 1:2], 1.0, None, ALU.mult))
            link(ts(inchunk[:, 0:1], col_f[:, 1:2], -1.0, 1.0, ALU.mult, ALU.add))
            link(tt(neg_k[:, :], neg_q[:, :], same[:, :], ALU.mult))
            link(ts(neg_k[:, :], neg_k[:, :], -BIG, BIG, ALU.mult, ALU.add))
            link(ts(neg_q[:, :], neg_q[:, :], -1.0, 1.0, ALU.mult, ALU.add))
            link(tt(incl[:, :], neg_q[:, :], same[:, :], ALU.mult))
            ts(neg_q[:, :], incl[:, :], BIG, -BIG, ALU.mult, ALU.add).then_inc(s["consts"], 1)
            dve.wait_ge(s_small[0], 16)
            inv = (1.0 / (ROPE_THETA ** (np.arange(0, ROPE, 2, dtype=np.float32) / np.float32(ROPE)))).astype(np.float32)
            link(v.tensor_copy(ang[:, 2, :, 0], posi[:, :]))
            for j in range(HALF - 1, -1, -1):
                mark(ts(ang[:, 3, :, j], ang[:, 2, :, 0], float(inv[j]), None, ALU.mult))
            ch.wait(ch.n)
            MAGIC = 1.5 * 2.0 ** 23
            C1 = 6.28125
            C2 = float(np.float32(2 * np.pi - C1).astype(np.float32))
            C2 = float(np.frombuffer(np.uint32(np.float32(C2).view(np.uint32) & 0xFFFFF000).tobytes(), np.float32)[0])
            C3 = float(np.float32(2 * np.pi - C1 - C2))
            link(ts(ang[:, 4, :, :], ang[:, 3, :, :], float(1 / (2 * np.pi)), None, ALU.mult))
            link(ts(ang[:, 4, :, :], ang[:, 4, :, :], MAGIC, None, ALU.add))
            link(ts(ang[:, 4, :, :], ang[:, 4, :, :], -MAGIC, None, ALU.add))
            for c in (C1, C2, C3):
                link(stt(ang[:, 3, :, :], ang[:, 4, :, :], -c, ang[:, 3, :, :], ALU.mult, ALU.add))
            PI = float(np.nextafter(np.float32(np.pi), np.float32(0)))
            link(ts(ang[:, 0, :, :], ang[:, 3, :, :], PI, -PI, ALU.min, ALU.max))
            link(ts(ang[:, 5, :, :], ang[:, 3, :, :], float(np.pi / 2), None, ALU.add))
            link(ts(ang[:, 4, :, :], ang[:, 5, :, :], PI, -2 * np.pi, ALU.is_gt, ALU.mult))
            link(tt(ang[:, 5, :, :], ang[:, 5, :, :], ang[:, 4, :, :], ALU.add))
            ts(ang[:, 1, :, :], ang[:, 5, :, :], PI, -PI, ALU.min, ALU.max).then_inc(s["trig"], 1)

            def norm(n, row, split_T=True):
                dve.wait_ge(s["norm_r"], n + 1)
                dve.wait_ge(s_row[row % 2], 16 * (row // 2 + 1))
                for t in range(TT):
                    i = stt(hbuf[:, t, :], x[:, t, :], rinv[:, t:t + 1], rows[:, row % 2, :], ALU.mult, ALU.mult)
                    i.then_inc(s["norm_h"], 1)
                dve.wait_ge(s["norm_h"], TT * (n + 1))
                v.memset(ss[:, 0:1], 0.0).then_inc(row_used, 1)
                if n == 2 * L or not split_T:
                    return
                for t in range(TT):
                    dve.wait_ge(s["norm_hi"], TT * n + t + 1)
                    sl = slice(t * P, (t + 1) * P)
                    tt(aT_lo[:, :, sl], two(4 + 2 * t).rearrange("p (k n) -> p k n", k=KC),
                       aT_hi[:, :, sl].bitcast(F32), ALU.subtract).then_inc(s["norm_lo"], 1)

            def bc(ap, n):
                return ap.unsqueeze(2).to_broadcast([P, ap.shape[1], n])

            for l in range(L):
                base = (MIX0, MIX1)[l]
                done[0] = base
                norm(2 * l, 4 * l)
                upto(base, first["z"] + SPL - 1)
                link(v.memset(pad[:, :, 0:3], 0.0)) if False else None
                if l == 0:
                    dve.wait_ge(s_small[2], 16)
                    dve.wait_ge(s_small[3], 16)
                dve.wait_ge(s["g1_used"], 6 * (l + 1))
                dtb = adt[:, l, 1:2, :].to_broadcast([P, TT, H])
                link(tt(sp[:, 0, :, :], abr[:, :, 0:H], dtb, ALU.add))
                link(ts(sp[:, 5, :, :], sp[:, 0, :, :], -1.0, None, ALU.mult))
                tt(sp[:, 1, :, :], sp[:, 0, :, :], sp[:, 5, :, :], ALU.min).then_inc(s["g_ready"], 1)
                dve.wait_ge(s_small[4], 16 * (l + 1))
                dve.wait_ge(s_small[5], 16 * (l + 1))
                dve.wait_ge(s["lat_r"], 2 * (l + 1))
                for t in range(TT):
                    link(stt(lat[:, t, 0:QL], lat[:, t, 0:QL], lri[:, t, 0:1], lat_w[:, 0:QL], ALU.mult, ALU.mult))
                    stt(lat[:, t, QL:QL + KVL], lat[:, t, QL:QL + KVL], lri[:, t, 1:2], lat_w[:, QL:QL + KVL],
                        ALU.mult, ALU.mult).then_inc(s["lat_h"], 1)
                dve.wait_ge(s["g_ready"], 3 * l + 2)
                link(ts(sp[:, 0, :, :], sp[:, 0, :, :], 0.0, None, ALU.max))
                link(tt(sp[:, 0, :, :], sp[:, 0, :, :], sp[:, 3, :, :], ALU.add))
                link(ts(sp[:, 4, :, :], sp[:, 4, :, :], 1.0, None, ALU.add))
                link(v.reciprocal(beta[:, :, :], sp[:, 4, :, :]))
                stt(gl[:, :, :], sp[:, 0, :, :], -1.0, adt[:, l, 0:1, :].to_broadcast([P, TT, H]),
                    ALU.mult, ALU.mult).then_inc(s["g_ready"], 1)
                upto(base, first["wq"] + SPL - 1)
                for t in range(TT):
                    dve.wait_ge(s["lat_hi"], TT * l + t + 1)
                    sl = slice(t * P, (t + 1) * P)
                    tt(pT_lo[:, :, sl], two(6)[:, 0:LC * P].rearrange("p (k n) -> p k n", k=LC),
                       pT_hi[:, :, sl].bitcast(F32), ALU.subtract).then_inc(s["lat_lo"], 1)
                upto(base, first["qkv"] + 2)

                def rope(dst1, dst2, t1, t2, cos, sin, u):
                    link(tt(tmp_r[:, 0, 0:u, :], t1, sin, ALU.mult))
                    link(tt(tmp_r[:, 1, 0:u, :], t2, sin, ALU.mult))
                    link(tt(dst1, t1, cos, ALU.mult))
                    link(tt(dst2, t2, cos, ALU.mult))
                    link(tt(dst1, dst1, tmp_r[:, 1, 0:u, :], ALU.subtract))
                    return tt(dst2, dst2, tmp_r[:, 0, 0:u, :], ALU.add)

                if l == 0:
                    dve.wait_ge(s["trig"], 3)
                dve.wait_ge(s["q_copied"], TT * (l + 1))
                for t in range(TT):
                    c, sn = (b[:, t:t + 1, :].to_broadcast([P, HM, HALF]) for b in (cosb, sinb))
                    t1, t2 = qm[:, t, :, NOPE:NOPE + HALF], qm[:, t, :, NOPE + HALF:DQ]
                    rope(t1, t2, t1, t2, c, sn, HM).then_inc(s["q_rope"], 1)
                    dve.wait_ge(s["q_rope"], TT * l + t + 1)
                for t in range(TT):
                    c, sn = (b[:, t:t + 1, :] for b in (cosb, sinb))
                    t1, t2 = krr[:, t:t + 1, 0:HALF], krr[:, t:t + 1, HALF:ROPE]
                    link(rope(t1, t2, t1, t2, c, sn, 1))
                    v.tensor_copy(km[:, t, :, NOPE:DQ], krr[:, t:t + 1, :].to_broadcast([P, HM, ROPE])
                                  ).then_inc(s["k_rope"], 1)

                def scores(u):
                    nh, nk = (HM, P) if u == 0 else (HM // 2, T)
                    dve.wait_ge(s["sc_done"], 3 * l + u + 1)
                    sc = two(3).rearrange("p (h n) -> p h n", n=nk)
                    link(v.memset(sc[0:CHUNK, :, nk - CHUNK:nk], -BIG))
                    link(v.tensor_reduce(mx[:, u, 0:nh], sc, AX_X, ALU.max))
                    ts(mx[:, u, 0:nh], mx[:, u, 0:nh], -(float(DQ) ** -0.5), None, ALU.mult
                       ).then_inc(s["sc_masked"], 1)

                def outs(u):
                    h0, nh, t = (0, HM, 0) if u == 0 else ((u - 1) * HM // 2, HM // 2, 1)
                    dve.wait_ge(s["pv_done"], 3 * l + u + 1)
                    link(v.reciprocal(ri[:, u, 0:nh], rs[:, u, 0:nh]))
                    i = tt(om[:, t, h0 * VD:(h0 + nh) * VD].rearrange("p (h d) -> p h d", h=nh),
                           ps[:, 7, h0 * VD:(h0 + nh) * VD].rearrange("p (h d) -> p h d", h=nh),
                           bc(ri[:, u, 0:nh], VD), ALU.mult)
                    i.then_inc(s["o_norm"], 1) if u != 1 else link(i)
                    if u == 1:
                        return

                upto(base, first["qkv"] + 10)
                scores(0)
                upto(base, first["qkv"] + 12)
                scores(1)
                upto(base, first["qkv"] + 14)
                outs(0)
                scores(2)
                upto(base, first["qkv"] + 16)
                outs(1)
                v.memset(sums[:, 48:49], 0.0).then_inc(s["x_ready"], 1)
                outs(2)
                upto(base, first["gate"] + 3)
                for t in range(TT):
                    dve.wait_ge(s["om_hi"], TT * l + t + 1)
                    sl = slice(t * P, (t + 1) * P)
                    tt(oT_lo[:, :, sl], ps[:, 4 + t, :].rearrange("p (k n) -> p k n", n=P),
                       oT_hi[:, :, sl].bitcast(F32), ALU.subtract).then_inc(s["om_lo"], 1)
                v.memset(pad[:, :, 0:3], 0.0).then_inc(s["pad_ready"], 1)
                if l == 0:
                    dve.wait_ge(s["cw_ready"], L)
                prev = [None] * NQK
                for k in range(1, CONV):
                    for c in range(NQK):
                        if k == 1:
                            dve.wait_ge(s["tap0"], NQK * l + c + 1)
                        else:
                            ch.wait(prev[c])
                        prev[c] = mark(stt(qkv[:, c, :], pad[:, c, k:k + T], cw[:, l, k, c:c + 1], qkv[:, c, :],
                                           ALU.mult, ALU.add))
                ch.wait(ch.n)
                v.memset(sums[:, 49:50], 0.0).then_inc(s["conv_done"], 1)
                upto(base, first["gate"] + 4)
                upto(base, first["gate"] + 7)
                dve.wait_ge(s["sums_done"], l + 1)
                v.tensor_copy(sums[:, 0:48], ps[:, 7, 0:48]).then_inc(s["sums_used"], 1)
                dve.wait_ge(s["sums_used"], l + 1)
                dve.wait_ge(s["lnrow"], l + 1)
                G, GL = (sums[:, j:j + 8].rearrange("p (t h) -> p t h", t=TT) for j in (16, 24))
                link(ts(gcol[:, 2, :, :], gcol[:, 0, :, :], -0.5, float(np.log(float(DV) ** -0.5)), ALU.mult, ALU.add))
                link(ts(gcol[:, 3, :, :], gcol[:, 1, :, :], 0.5, None, ALU.mult))
                link(tt(gcol[:, 4, :, :], G, gcol[:, 3, :, :], ALU.subtract))
                link(tt(gcol[:, 5, :, :], G, gcol[:, 3, :, :], ALU.add))
                link(ts(gcol[:, 5, :, :], gcol[:, 5, :, :], -1.0, None, ALU.mult))
                tt(gcol[:, 6, :, :], GL, gcol[:, 5, :, :], ALU.add).then_inc(s["lncols"], 1)
                dve.wait_ge(s["cols_ready"], l + 1)
                link(tt(gcol[:, 9, :, :], gcol[:, 7, :, :], beta[:, :, :], ALU.mult))
                upto(base, first["gate"] + 8)
                for t in range(TT):
                    dve.wait_ge(s["row_exp"], TT * l + t + 1)
                    link(tt(inT[:, t, :].rearrange("p (h n) -> p h n", h=H),
                            ps[:, 4 + t, :].rearrange("p (h n) -> p h n", h=H),
                            neg_q[:, :].unsqueeze(1).to_broadcast([P, H, P]), ALU.add))
                    tt(Lm[:, t, :].rearrange("p (h n) -> p h n", h=H),
                       ps[:, 6 + t, :].rearrange("p (h n) -> p h n", h=H),
                       neg_k[:, :].unsqueeze(1).to_broadcast([P, H, P]), ALU.add).then_inc(s["eq_in"], 1)
                for t in range(TT):
                    sl = slice(t * P, (t + 1) * P)
                    link(tt(qdT[:, :, sl], qdT[:, :, sl], qkv[:, 0:H, sl], ALU.mult))
                for t in range(TT):
                    dve.wait_ge(s["kk_done"], TT * l + t + 1)
                    dve.wait_ge(s["e_exp"], 16 * l + 8 * (t + 1))
                    for h in range(H):
                        hs = slice(h * P, (h + 1) * P)
                        mark(stt(Lm[:, t, hs], Lm[:, t, hs], beta[:, t, h:h + 1], ps[:, 4 + t, hs],
                                 ALU.mult, ALU.mult))
                    mark(tt(inT[:, t, :], inT[:, t, :], ps[:, 6 + t, :], ALU.mult))
                    ch.wait(ch.n)
                    v.memset(sums[:, 50:51], 0.0).then_inc(s["L_ready"], 1)
                upto(base, first["gate"] + 9)
                for t in range(TT):
                    dve.wait_ge(s["kt_done"], 2 * TT * l + t + 1)
                    kp = ps[:, 6 + t, :].rearrange("p (h n) -> p h n", h=H)
                    mark(tt(kb[:, t, :].rearrange("p (h n) -> p h n", h=H), kp, bc(gcol[:, 9, t, :], P), ALU.mult))
                    tt(kd[:, t, :].rearrange("p (h n) -> p h n", h=H), kp, bc(gcol[:, 8, t, :], P),
                       ALU.mult).then_inc(s["kt_used"], 1)
                m3 = lambda m: m.unsqueeze(1).to_broadcast([P, H, P])
                r3 = lambda b, t: b[:, t, :].rearrange("p (h n) -> p h n", h=H)
                for t in range(TT):
                    dve.wait_ge(s["LT_ready"], TT * l + t + 1)
                    link(tt(r3(X, t), r3(Lm, t), m3(lev0[:, :]), ALU.mult))
                    link(tt(r3(X, t), m3(ident[:, :]), r3(X, t), ALU.subtract))
                    link(tt(r3(XT, t), r3(LT, t), m3(lev[:, 0, :]), ALU.mult))
                    link(tt(r3(XT, t), m3(ident[:, :]), r3(XT, t), ALU.subtract))
                    tt(r3(MT, t), r3(LT, t), m3(lev[:, 1, :]), ALU.mult).then_inc(s["inv_ready"], 1)
                for t in range(TT):
                    dve.wait_ge(s["kt_done"], 2 * TT * l + TT + t + 1)
                    tt(r3(vb, t), ps[:, 6 + t, :].rearrange("p (h n) -> p h n", h=H), bc(beta[:, t, :], P),
                       ALU.mult).then_inc(s["kt_used"], 1)

                def gate_bias(hf):
                    r = 4 * l + 1 + hf
                    dve.wait_ge(w_used, base + first["gate"] + KC * (hf + 1))
                    dve.wait_ge(s_row[r % 2], 16 * (r // 2 + 1))
                    for t in range(TT):
                        tt(gates[:, t, hf * D:(hf + 1) * D], two(2 * t), rows[:, r % 2, :], ALU.add
                           ).then_inc(s["gate_in"], 1)
                    dve.wait_ge(s["gate_in"], 4 * l + 2 * (hf + 1))
                    v.memset(sums[:, 51:52], 0.0).then_inc(row_used, 1)

                for k in range(1, NLEV):
                    upto(base, first["gate"] + 10 + k)
                    if k == 1:
                        gate_bias(0)
                    for t in range(TT):
                        n = (5 * l + k - 1) * TT + t + 1
                        dve.wait_ge(s["zz_done"], n)
                        if k < NLEV - 1:
                            mark(tt(r3(X, t), r3(X, t), ps[:, 6, :].rearrange("p (h n) -> p h n", h=H), ALU.subtract))
                            mark(tt(r3(MT, t), r3(LT, t), m3(lev[:, k + 1, :]), ALU.mult))
                        mark(tt(r3(XT, t), r3(XT, t), ps[:, 7, :].rearrange("p (h n) -> p h n", h=H), ALU.subtract))
                        ch.wait(ch.n)
                        v.memset(sums[:, 50:51], 0.0).then_inc(s["inv_ready"], 1)
                        dve.wait_ge(s["inv_ready"], TT * l * 6 + TT + (k - 1) * TT + t + 1)
                upto(base, first["gate"] + 16)
                dve.wait_ge(s["w_done"], TT * (l + 1))
                for t in range(TT):
                    link(v.tensor_copy(ub[:, t, :], ps[:, 6 + t, :]))
                v.memset(sums[:, 50:51], 0.0).then_inc(s["u_ready"], 1)
                for c in range(4):
                    t, r = c // 2, slice((c % 2) * CHUNK, (c % 2 + 1) * CHUNK)
                    if c:
                        dve.wait_ge(s["v_done"], 3 * l + c)
                        tt(vnb[r, t, :], ub[r, t, :], ps[r, 4, :], ALU.subtract).then_inc(s["vn_ready"], 1)
                        if c < 3:
                            link(tt(r3(S, c % 2), r3(S, 1 - c % 2), bc(cdb[:, c, :], P), ALU.mult))
                    else:
                        v.tensor_copy(vnb[r, t, :], ub[r, t, :]).then_inc(s["vn_ready"], 1)
                    if c < 3:
                        dve.wait_ge(s["s_done"], 3 * l + c + 1)
                        if c == 0:
                            v.tensor_copy(S[:, 0, :], ps[:, 5, :]).then_inc(s["s_ready"], 1)
                        else:
                            tt(S[:, c % 2, :], S[:, c % 2, :], ps[:, 5, :], ALU.add).then_inc(s["s_ready"], 1)
                        dve.wait_ge(s["s_ready"], 3 * l + c + 1)
                og, osq = X, XT
                for t in range(TT):
                    dve.wait_ge(s["o_done"], 4 * l + 2 * (t + 1))
                    link(v.tensor_copy(og[:, t, :], ps[:, 6 + t, :]))
                    link(tt(osq[:, t, :], og[:, t, :], og[:, t, :], ALU.mult))
                    v.tensor_reduce(oss[:, t, :], r3(osq, t), AX_X, ALU.add).then_inc(s["o_ss"], 1)
                dve.wait_ge(s_small[6], 16 * (l + 1))
                for t in range(TT):
                    link(tt(r3(zs, t), r3(zs, t), onorm[:, :].unsqueeze(1).to_broadcast([P, H, P]), ALU.mult)
                         ) if t else (dve.wait_ge(s["z_ready"], TT * (l + 1)),
                                      link(tt(r3(zs, t), r3(zs, t),
                                              onorm[:, :].unsqueeze(1).to_broadcast([P, H, P]), ALU.mult)))
                dve.wait_ge(s["o_r"], l + 1)
                for t in range(TT):
                    link(tt(r3(og, t), r3(og, t), bc(ori[:, t, :], P), ALU.mult))
                    tt(og[:, t, :], og[:, t, :], zs[:, t, :], ALU.mult).then_inc(s["og_ready"], 1)
                upto(base, first["gdn_o"] + 3)
                for t in range(TT):
                    dve.wait_ge(s["og_hi"], TT * l + t + 1)
                    sl = slice(t * P, (t + 1) * P)
                    tt(pT_lo[:, 0:H, sl], ps[:, 4 + t, :].rearrange("p (k n) -> p k n", n=P),
                       pT_hi[:, 0:H, sl].bitcast(F32), ALU.subtract).then_inc(s["og_lo"], 1)
                gate_bias(1)
                upto(base, first["mla_o"] + 3)
                dve.wait_ge(w_used, base + first["mla_o"])
                dve.wait_ge(s["gate_ready"], 4 * (l + 1))
                for t in range(TT):
                    tt(gates[:, t, 0:D], gates[:, t, 0:D], two(2 * t), ALU.mult).then_inc(s["oa_in"], 1)
                upto(base, first["out"] + 2)
                dve.wait_ge(w_used, base + first["out"])
                for t in range(TT):
                    link(tt(gates[:, t, D:2 * D], gates[:, t, D:2 * D], two(4 + 2 * t), ALU.mult))
                    tt(hbuf[:, t, :], gates[:, t, 0:D], gates[:, t, D:2 * D], ALU.add).then_inc(s["merged"], 1)
                for t in range(TT):
                    dve.wait_ge(s["m_hi"], TT * l + t + 1)
                    sl = slice(t * P, (t + 1) * P)
                    tt(aT_lo[:, :, sl], two(2 * t).rearrange("p (k n) -> p k n", k=KC),
                       aT_hi[:, :, sl].bitcast(F32), ALU.subtract).then_inc(s["m_lo"], 1)
                upto(base, N_MIX)
                dve.wait_ge(w_used, base + N_MIX)
                for t in range(TT):
                    tt(x[:, t, :], x[:, t, :], two(4 + 2 * t), ALU.add).then_inc(s["x_new"], 1)
                dve.wait_ge(s["x_new"], 2 * TT * l + TT)

                if l == 0:
                    norm(1, 3)

                    def transposed(i, d, k0):
                        for t in range(TT):
                            dve.wait_ge(s["hT_hi"], At(t + 1 - d * TT, i, TT).count())
                            tt(dT_lo[:, bass.ds(k0, 7), t * P:(t + 1) * P],
                               two(4 + 2 * t)[:, 0:2 * SUB].rearrange("p (k n) -> p k n", n=P),
                               dT_hi[:, bass.ds(k0, 7), t * P:(t + 1) * P].bitcast(F32),
                               ALU.subtract).then_inc(s["hT_lo"], 1)

                    def up(i):
                        for j in range(N_UP):
                            split(At(DENSE + j, i, N_UP), 2 * SUB)
                            if j == 3 + SPL and i is not None:
                                transposed(i, 1, i * 7 - 7)
                            if j in (10, 15):
                                sub = j // 12
                                dve.wait_ge(w_used, At(DENSE + 8 * sub + 8, i, N_UP).count())
                                dve.wait_ge(s["h1_used"], At(sub + 1, i, 2).count())
                                tt(dhid[:, :, sub * SUB:(sub + 1) * SUB], dsil[:, sub, :, :], ps[:, 2:4, 0:SUB],
                                   ALU.mult).then_inc(s["h3_used"], 1)

                    up(None)
                    with dve.Fori(1, UPS) as i:
                        up(i)
                    split(At(MIX1 - N_DOWN), D)
                    transposed(None, 1 - UPS, N_DOWN - 7)
                    for k in range(1, N_DOWN):
                        split(At(DENSE + UPS * N_UP + k), D)
                    dve.wait_ge(w_used, MIX1)
                    for t in range(TT):
                        tt(x[:, t, :], x[:, t, :], two(2 * t), ALU.add).then_inc(s["x_new"], 1)
                    dve.wait_ge(s["x_new"], 2 * TT)
                else:
                    norm(3, 7, False)
                    for t in range(TT):
                        link(v.tensor_copy(y_hi[:, 0:2].bitcast(F32), hbuf[:, t, 0:2])) if False else None
                        v.memset(cmax[:, 0:1], 0.0).then_inc(s["sel_in"], 1)
                        dve.wait_ge(s["sel_in"], t + 1)
                    dve.wait_ge(s["lg_done"], 1)
                    link(v.tensor_copy(lg[:, :, :], ps[:, 0, 0:TT * NE].rearrange("p (t e) -> p t e", t=TT)))
                    for t in range(TT):
                        link(v.max(top[:, t, :], lg[:, t, :]))
                        link(v.max_index(topi[:, t, :], top[:, t, :], lg[:, t, :]))
                    link(v.tensor_copy(topf[:, :, :], topi[:, :, 0:TOP_K]))
                    for k in range(TOP_K):
                        for t in range(TT):
                            link(ts(oneh[:, k, t, :], slot_no[:, 0, 0:NE], -1.0, topf[:, t, k:k + 1],
                                    ALU.add, ALU.is_equal))
                    link(tt(mask[:, :, :], oneh[:, 0, :, :], oneh[:, 1, :, :], ALU.add))
                    tt(tw[:, :, 0:1], top[:, :, 1:2], top[:, :, 0:1], ALU.subtract).then_inc(s["lg_ready"], 1)
                    for t in range(TT):
                        dve.wait_ge(s["e_ready"], t + 1)
                        mark(tt(h2_lo[:, t, :], hbuf[:, t, :], h2_hi[:, t, :].bitcast(F32), ALU.subtract))
                    dve.wait_ge(s["e_ready"], TT + 1)
                    link(ts(tw[:, :, 2:3], tw[:, :, 1:2], 1.0, None, ALU.add))
                    link(v.reciprocal(tw[:, :, 2:3], tw[:, :, 2:3]))
                    link(tt(tw[:, :, 3:4], tw[:, :, 1:2], tw[:, :, 2:3], ALU.mult))
                    for t in range(TT):
                        w = comb[:, t, 1:NE + 1]
                        link(v.memset(comb[:, t, 0:1], 0.0))
                        link(v.memset(rank[:, t, NE:NE + 1], 0.0))
                        link(ts(w, oneh[:, 0, t, :], tw[:, t, 2:3], None, ALU.mult))
                        link(stt(w, oneh[:, 1, t, :], tw[:, t, 3:4], w, ALU.mult, ALU.add))
                    link(v.memset(y_hi[:, :].bitcast(F32), 0.0))
                    link(v.memset(y_lo[:, :].bitcast(F32), 0.0))
                    link(v.memset(selT[:, :].bitcast(F32), 0.0))
                    dve.wait_ge(s["rank_done"], 1)
                    pr = ps[:, 1, 0:3 * NE].rearrange("p (t e) -> p t e", t=3)
                    rk = rank[:, :, 0:NE]
                    link(ts(rk, pr[:, 0:2, :], 1.0, None, ALU.add))
                    link(v.tensor_reduce(cmax[:, 0:1], pr[:, 2, :], AX_X, ALU.max))
                    link(tt(rk, rk, mask[:, :, :], ALU.mult))
                    v.memset(cmax[:, 1:2], 0.0).then_inc(s["rank_ready"], 1)
                    ts(flag[:, :], cmax[:, 0:1], float(P), None, ALU.is_gt).then_inc(s["rank_ready"], 1)
                    dve.wait_ge(s["rank_ready"], 2)

                    def select(e, c, r, per):
                        for t in range(TT):
                            i = ts(sel[:, t, :], slot_no[:, r, :], rank[:, t, c], None, ALU.is_equal)
                            i.then_inc(s["sel_ready"], 1)

                    def back(e, c, t, col):
                        dve.wait_ge(s["sct_done"], c)
                        stt(x[:, t, :], two(6), comb[:, t, col], x[:, t, :], ALU.mult, ALU.add
                            ).then_inc(s["sct_used"], 1)

                    def experts(base, r):
                        select(None, slice(0, 1), r, 0)
                        with dve.Fori(0, NE) as e:
                            def halves(c):
                                return At(8 + 16 * r + c, e, 2).count()

                            for j in range(N_EXP):
                                split(At(base + j, e, N_EXP), EXP_COLS[j])
                                if j in (7, 11):
                                    t = j // 8
                                    if t == 0:
                                        dve.wait_ge(s["x_new"], 3 * TT)
                                    back(e, At(18 * r + t + 1, e, 2).count(), t, bass.ds(e, 1))
                                if j == 16:
                                    dve.wait_ge(s["selT_done"], At(8 * r + 1, e, 1).count())
                                    select(e, bass.ds(e + 1, 1), r, 2)
                                if j in (19, 35):
                                    hf = j // 32
                                    dve.wait_ge(w_used, At(base + (2 * hf + 2) * KC, e, N_EXP).count())
                                    dve.wait_ge(s["h1_used"], halves(hf + 1))
                                    tt(ehid[:, hf * HC:(hf + 1) * HC].rearrange("p (a n) -> p a n", a=2),
                                       esil[:, :].rearrange("p (a n) -> p a n", a=2), ps[:, 2:4, 0:HC // 2],
                                       ALU.mult).then_inc(s["h3_used"], 1)
                                if j in (23, 38):
                                    hf = j // 32
                                    dve.wait_ge(s["hT_hi"], halves(hf + 1))
                                    cs = slice(hf * EC // 2, (hf + 1) * EC // 2)
                                    tt(eT_lo[:, cs, :], two(6)[:, 0:HC].rearrange("p (k n) -> p k n", n=P),
                                       eT_hi[:, cs, :].bitcast(F32), ALU.subtract).then_inc(s["hT_lo"], 1)
                            dve.wait_ge(s["ey_hi"], At(8 * r + 1, e, 1).count())
                            tt(y_lo[:, :], two(4), y_hi[:, :].bitcast(F32), ALU.subtract).then_inc(s["ey_lo"], 1)
                        for t in range(TT):
                            back(None, 18 * r + 2 * NE + t + 1, t, slice(NE, NE + 1))
                        dve.wait_ge(s["sct_used"], 18 * (r + 1))

                    ch.wait(ch.n)
                    experts(MOE, 0)
                    over = dve.value_load(flag[0:1, 0:1], min_val=0, max_val=1)
                    with dve.If(over):
                        experts(OVER, 1)
                    v.memset(cmax[:, 1:2], 0.0).then_inc(s["over_done"], 1)
                    norm(2 * L, 8)

        @block.tensor
        def _(pe):
            mm = nc.tensor.matmul

            def prod(o, hi, lo, rhi, rlo, start, stop, skip=False):
                mm(o, hi, rhi, start=start, stop=False, skip_group_check=skip)
                mm(o, hi, rlo, start=False, stop=False, skip_group_check=skip)
                return mm(o, lo, rhi, start=False, stop=stop, skip_group_check=skip)

            def tile(t, n, c0=0):
                pe.wait_ge(w_lo, t.count(1))
                sl = t.c % SPL
                return whi[:, sl, c0:c0 + n], wlo[:, sl, c0:c0 + n]

            def by_token(base, name, j0, n, lhs, cols, bank, signal=None, K=None):
                K = K or n
                for j in range(j0, j0 + n):
                    T_ = At(base + first[name] + j)
                    whs, wls = tile(T_, sum(cols))
                    k = j % K
                    last = None
                    for t in range(TT):
                        c = 0
                        for b, w in enumerate(cols):
                            sl = slice(t * P, (t + 1) * P)
                            last = prod(ps[:, bank + 2 * t + b, 0:w], lhs[0][:, k, sl], lhs[1][:, k, sl],
                                        whs[:, c:c + w], wls[:, c:c + w], k == 0, k == K - 1)
                            c += w
                    last.then_inc(w_used, 1)
                return last

            def transposes(o, src, n, w=P):
                for k in range(n):
                    last = nc.tensor.transpose(o[0:w, k * P:(k + 1) * P], src[:, k * w:(k + 1) * w], ident[:, :])
                return last

            def norm(n):
                for t in range(TT):
                    pe.wait_ge(s["norm_h"], TT * n + t + 1)
                    transposes(two(4 + 2 * t), hbuf[:, t, :], KC).then_inc(s["norm_T"], 1)

            pe.wait_ge(s["consts"], 1)
            pe.wait_ge(s_small[1], 16)
            for l in range(L):
                nc.tensor.transpose(ps[:, l, 0:CONV * NQK], cw_in[:, l, :],
                                    ident[0:CONV * NQK, 0:CONV * NQK]).then_inc(s["cwT"], 1)
            pe.wait_ge(s["cw_ready"], L)

            for l in range(L):
                base = (MIX0, MIX1)[l]
                aT, pT, oT = (aT_hi, aT_lo), (pT_hi, pT_lo), (oT_hi, oT_lo)
                norm(2 * l)
                pe.wait_ge(s["norm_lo"], TT * (2 * l + 1))
                if l:
                    pe.wait_ge(s["x_new"], 2 * TT * l)
                by_token(base, "g1", 0, KC, aT, [512, G1 - 512], 0)
                for j in range(KC):
                    whs, wls = tile(At(base + first["z"] + j), QW)
                    for t in range(TT):
                        sl = slice(t * P, (t + 1) * P)
                        last = prod(ps[:, 4 + t, :], aT_hi[:, j, sl], aT_lo[:, j, sl], whs, wls, j == 0, j == KC - 1)
                    last.then_inc(w_used, 1)
                for t in range(TT):
                    pe.wait_ge(s["lat_h"], TT * l + t + 1)
                    if t:
                        pe.wait_ge(s["lat_lo"], TT * l + t)
                    transposes(two(6), lat[:, t, :], LC).then_inc(s["lat_T"], 1)
                pe.wait_ge(s["lat_lo"], TT * (l + 1))
                pe.wait_ge(s["z_ready"], TT * (l + 1))
                by_token(base, "wq", 0, QC, pT, [512, QN - 512], 4)
                pe.wait_ge(s["g1_used"], 6 * (l + 1))
                kv = (pT_hi[:, QC:LC, :], pT_lo[:, QC:LC, :])
                by_token(base, "wkv", 0, LC - QC, kv, [512, 512], 0)
                pe.wait_ge(s["q_copied"], TT * (l + 1))
                pe.wait_ge(s["kv_copied"], 2 * TT * (l + 1))

                def qkv_tiles(j0, n):
                    for j in range(j0, j0 + n):
                        hf, k = j // KC, j % KC
                        if j == KC:
                            pe.wait_ge(s["pad_ready"], 3 * l + 1)
                        whs, wls = tile(At(base + first["qkv"] + j), 3 * QW // 2)
                        for c in range(NQK // 2):
                            cs = slice(c * P, (c + 1) * P)
                            o = ps[:, c // 2, (c % 2) * T:(c % 2 + 1) * T]
                            last = prod(o, whs[:, cs], wls[:, cs], aT_hi[:, k, :], aT_lo[:, k, :],
                                        k == 0 and c % 2 == 0, k == KC - 1, True)
                        last.then_inc(w_used, 1)

                def qk_T(u):
                    src = (qm, km)[u // 2]
                    if u < 2:
                        pe.wait_ge(s["q_rope"], TT * l + u % 2 + 1)
                    else:
                        pe.wait_ge(s["k_rope"], TT * l + u % 2 + 1)
                        pe.wait_ge(s["qk_Tc"], 4 * l + u - 1)
                    o = two(4 + 2 * (u % 2))
                    for h in range(HM):
                        last = nc.tensor.transpose(o[0:DQ, h * P:(h + 1) * P], src[:, u % 2, h, :], ident[:, :])
                    last.then_inc(s["qk_T"], 1)

                def scores(u):
                    nh, nk, t = (HM, P, 0) if u == 0 else (HM // 2, T, 1)
                    if u:
                        pe.wait_ge(s["sc_exp"], 16 * l + (0, 8, 12)[u])
                    for h in range(nh):
                        hh = h + (HM // 2 if u == 2 else 0)
                        last = mm(two(3)[:, h * nk:(h + 1) * nk], qT[:, hh, t * P:(t + 1) * P], kT[:, hh, 0:nk],
                                  start=True, stop=True)
                    last.then_inc(s["sc_done"], 1)

                def p_T(u):
                    pe.wait_ge(s["sc_exp"], 16 * l + (8, 12, 16)[u])
                    if u:
                        pe.wait_ge(s["p_Tc"], 3 * l + u)
                    transposes(two(5), prob[:, u % 2, :], KC).then_inc(s["p_T"], 1)

                def pv(u):
                    nh, nk, h0 = (HM, 1, 0) if u == 0 else (HM // 2, TT, (u - 1) * HM // 2)
                    pe.wait_ge(s["p_Tc"], 3 * l + u + 1)
                    if u == 1:
                        pe.wait_ge(s["o_norm"], 2 * l + 1)
                    if u == 2:
                        pe.wait_ge(s["x_ready"], (l + 1) * 1)
                    for h in range(nh):
                        for k in range(nk):
                            c = h * nk + k
                            last = mm(ps[:, 7, (h0 + h) * VD:(h0 + h + 1) * VD], probT[:, u % 2, c * P:(c + 1) * P],
                                      vm[:, k, (h0 + h) * VD:(h0 + h + 1) * VD], start=(k == 0), stop=(k == nk - 1))
                    last.then_inc(s["pv_done"], 1)

                qkv_tiles(0, 4)
                qk_T(0)
                qk_T(1)
                qkv_tiles(4, 2)
                qk_T(2)
                qk_T(3)
                qkv_tiles(6, 2)
                pe.wait_ge(s["qk_Tc"], 4 * (l + 1))
                scores(0)
                qkv_tiles(8, 2)
                p_T(0)
                scores(1)
                qkv_tiles(10, 2)
                pv(0)
                p_T(1)
                scores(2)
                qkv_tiles(12, 2)
                pv(1)
                p_T(2)
                qkv_tiles(14, 2)
                pv(2)

                def gate_tiles(j0, n):
                    for j in range(j0, j0 + n):
                        if j == 0:
                            pe.wait_ge(s["pad_ready"], 3 * l + 2)
                            pe.wait_ge(s["sc_exp"], 16 * (l + 1))
                        if j == KC:
                            pe.wait_ge(s["gate_in"], 4 * l + 2)
                        by_token(base, "gate", j, 1, aT, [512, 512], 0, K=KC)

                gate_tiles(0, 1)
                pe.wait_ge(s["o_norm"], 2 * (l + 1))
                for t in range(TT):
                    transposes(ps[:, 4 + t, :], om[:, t, :], MV // P).then_inc(s["om_T"], 1)
                gate_tiles(1, 3)
                pe.wait_ge(s["g_ready"], 3 * (l + 1))
                pe.wait_ge(s["sq_ready"], 2 * (l + 1))
                pe.wait_ge(s["om_lo"], TT * (l + 1))
                sq = (X, XT)
                for j in range(2):
                    for t in range(TT):
                        for h in range(H):
                            c = j * 8 + t * 4 + h
                            src = sq[j][:, :, :].rearrange("p a b -> p (a b)")[:, h * T + t * P:h * T + (t + 1) * P]
                            mm(ps[:, 7, c:c + 1], src, ones[:, 0:1], start=True, stop=True)
                for t in range(TT):
                    mm(ps[:, 7, 16 + 4 * t:20 + 4 * t], incl[:, :], gl[:, t, :], start=True, stop=True)
                    mm(ps[:, 7, 24 + 4 * t:28 + 4 * t], same[:, :], gl[:, t, :], start=True, stop=True)
                for c in range(4):
                    last = mm(ps[:, 7, 32 + 4 * c:36 + 4 * c], inchunk[:, c % 2:c % 2 + 1].to_broadcast([P, P]),
                              gl[:, c // 2, :], start=True, stop=True)
                last.then_inc(s["sums_done"], 1)
                gate_tiles(4, 1)
                pe.wait_ge(s["lncols"], l + 1)
                for t in range(TT):
                    for j in range(2):
                        for h in range(H):
                            o = ps[:, 4 + 2 * j + t, h * P:(h + 1) * P]
                            mm(o, gl[:, t, h:h + 1].to_broadcast([P, P]), incl[:, :], start=True, stop=False)
                            last = mm(o, gcol[:, 2 + j, t, h:h + 1].to_broadcast([P, P]), ident[:, :],
                                      start=False, stop=True)
                    last.then_inc(s["row_done"], 1)
                for t in range(TT):
                    pe.wait_ge(s["eq_in"], TT * l + t + 1)
                    sl = slice(t * P, (t + 1) * P)
                    for h in range(H):
                        mm(ps[:, 4 + t, h * P:(h + 1) * P], qkv[:, H + h, sl], qkv[:, H + h, sl], start=True, stop=True)
                        last = mm(ps[:, 6 + t, h * P:(h + 1) * P], qkv[:, H + h, sl], qkv[:, h, sl],
                                  start=True, stop=True)
                    last.then_inc(s["kk_done"], 1)
                gate_tiles(5, 1)
                for t in range(TT):
                    pe.wait_ge(s["L_ready"], TT * l + t + 1)
                    transposes(ps[:, 4 + t, :], Lm[:, t, :], H).then_inc(s["LT_done"], 1)
                for t in range(TT):
                    for h in range(H):
                        last = nc.tensor.transpose(ps[:, 6 + t, h * P:(h + 1) * P], qkv[:, H + h, t * P:(t + 1) * P],
                                                   ident[:, :])
                    last.then_inc(s["kt_done"], 1)
                for t in range(TT):
                    pe.wait_ge(s["kt_used"], 2 * TT * l + t + 1)
                    for h in range(H):
                        last = nc.tensor.transpose(ps[:, 6 + t, h * P:(h + 1) * P], qkv[:, 2 * H + h, t * P:(t + 1) * P],
                                                   ident[:, :])
                    last.then_inc(s["kt_done"], 1)
                gate_tiles(6, 2)
                for k in range(1, NLEV):
                    if k > 1:
                        gate_tiles(6 + k, 1)
                    for t in range(TT):
                        pe.wait_ge(s["inv_ready"], TT * l * 6 + (k - 1) * TT + t + 1)
                        if k == 1:
                            pe.wait_ge(s["LT_ready"], TT * l + t + 1)
                            pe.wait_ge(s["kt_used"], 2 * TT * (l + 1))
                        for h in range(H):
                            hs = slice(h * P, (h + 1) * P)
                            last = mm(ps[:, 4 + t, hs], MT[:, t, hs], X[:, t, hs], start=True, stop=True)
                        last.then_inc(s["y_done"], 1)
                    for t in range(TT):
                        pe.wait_ge(s["y_ready"], (5 * l + k - 1) * TT + t + 1)
                        if t:
                            pe.wait_ge(s["inv_ready"], TT * l * 6 + TT + (k - 1) * TT + t)
                        for h in range(H):
                            hs = slice(h * P, (h + 1) * P)
                            if k < NLEV - 1:
                                mm(ps[:, 6, hs], XT[:, t, hs], Lm[:, t, hs], start=True, stop=True)
                            last = mm(ps[:, 7, hs], Lm[:, t, hs], XT[:, t, hs], start=True, stop=True)
                        last.then_inc(s["zz_done"], 1)
                gate_tiles(12, 1)
                pe.wait_ge(s["inv_ready"], TT * (l + 1) * 6)
                for t in range(TT):
                    for h in range(H):
                        hs = slice(h * P, (h + 1) * P)
                        mm(ps[:, 4 + t, hs], kb[:, t, hs], XT[:, t, hs], start=True, stop=True)
                        last = mm(ps[:, 6 + t, hs], XT[:, t, hs], vb[:, t, hs], start=True, stop=True)
                    last.then_inc(s["w_done"], 1)
                for c in range(4):
                    t, r = c // 2, slice((c % 2) * CHUNK, (c % 2 + 1) * CHUNK)
                    tk = slice(c * CHUNK, (c + 1) * CHUNK)
                    if c == 0:
                        pe.wait_ge(s["w_ready"], TT * (l + 1))
                        pe.wait_ge(s["u_ready"], l + 1)
                    else:
                        pe.wait_ge(s["s_ready"], 3 * l + c)
                        for h in range(H):
                            hs = slice(h * P, (h + 1) * P)
                            last = mm(ps[r, 4, hs], wTb[:, h, tk], S[:, 1 - c % 2, hs], start=True, stop=True)
                        last.then_inc(s["v_done"], 1)
                        for h in range(H):
                            pass
                    if c < 3:
                        gate_tiles(13 + c, 1)
                    pe.wait_ge(s["vn_ready"], 4 * l + c + 1)
                    if c < 3:
                        for h in range(H):
                            hs = slice(h * P, (h + 1) * P)
                            last = mm(ps[:, 5, hs], kd[r, t, hs], vnb[r, t, hs], start=True, stop=True)
                        last.then_inc(s["s_done"], 1)
                    for h in range(H):
                        hs = slice(h * P, (h + 1) * P)
                        if c:
                            mm(ps[r, 6 + t, hs], qdT[:, h, tk], S[:, 1 - c % 2, hs], start=True, stop=False)
                        last = mm(ps[r, 6 + t, hs], inT[r, t, h * P + r.start:h * P + r.stop], vnb[r, t, hs],
                                  start=(c == 0), stop=True)
                    last.then_inc(s["o_done"], 1)
                for t in range(TT):
                    pe.wait_ge(s["og_ready"], TT * l + t + 1)
                    transposes(ps[:, 4 + t, :], X[:, t, :], H).then_inc(s["og_T"], 1)
                pe.wait_ge(s["gate_in"], 4 * (l + 1))
                pe.wait_ge(s["og_lo"], TT * (l + 1))
                by_token(base, "gdn_o", 0, H, pT, [512, 512], 0)
                by_token(base, "mla_o", 0, MV // P, oT, [512, 512], 4)
                pe.wait_ge(s["oa_in"], TT * (l + 1))
                for t in range(TT):
                    pe.wait_ge(s["merged"], TT * l + t + 1)
                    transposes(two(2 * t), hbuf[:, t, :], KC).then_inc(s["m_T"], 1)
                pe.wait_ge(s["m_lo"], TT * (l + 1))
                by_token(base, "out", 0, KC, aT, [512, 512], 4)

                if l == 0:
                    pe.wait_ge(s["x_new"], TT)
                    norm(1)
                    pe.wait_ge(s["norm_lo"], TT * 2)
                    def hidden_T(i, d):
                        pe.wait_ge(s["h3_used"], At(2 - 2 * d, i, 2).count())
                        for t in range(TT):
                            if i is not None and d == 1:
                                pass
                            transposes(two(4 + 2 * t), dhid[:, t, :], 7).then_inc(s["hT_done"], 1)

                    def up(i):
                        for sub in range(2):
                            for wi in range(2):
                                if wi == 1 and sub == 0 and i is not None:
                                    hidden_T(i, 1)
                                if sub:
                                    pe.wait_ge(s[("h1_used", "h3_used")[wi]], At(sub, i, 2).count())
                                elif i is not None and wi == 0:
                                    pe.wait_ge(s["h1_used"], At(0, i, 2).count())
                                for j in range(4):
                                    T_ = At(DENSE + sub * 8 + wi * 4 + j, i, N_UP)
                                    whs, wls = tile(T_, 2 * SUB)
                                    for a in range(2):
                                        k = 2 * j + a
                                        for t in range(TT):
                                            sl, cs = slice(t * P, (t + 1) * P), slice(a * SUB, (a + 1) * SUB)
                                            last = prod(ps[:, 2 * wi + t, 0:SUB], aT_hi[:, k, sl], aT_lo[:, k, sl],
                                                        whs[:, cs], wls[:, cs], k == 0, k == KC - 1)
                                    last.then_inc(w_used, 1)
                        if i is not None:
                            pe.wait_ge(s["hT_lo"], At(0, i, TT).count())

                    up(None)
                    with pe.Fori(1, UPS) as i:
                        up(i)
                    for k in range(N_DOWN):
                        if k == 1:
                            hidden_T(None, 1 - UPS)
                        if k == N_DOWN - 7:
                            pe.wait_ge(s["hT_lo"], TT * UPS)
                        whs, wls = tile(At(DENSE + UPS * N_UP + k), D)
                        for t in range(TT):
                            for b in range(2):
                                sl, cs = slice(t * P, (t + 1) * P), slice(b * 512, (b + 1) * 512)
                                last = prod(ps[:, 2 * t + b, :], dT_hi[:, k, sl], dT_lo[:, k, sl],
                                            whs[:, cs], wls[:, cs], k == 0, k == N_DOWN - 1)
                        last.then_inc(w_used, 1)
                else:
                    pe.wait_ge(s["x_new"], 3 * TT)
                    norm(3)
                    pe.wait_ge(s["norm_hi"], TT * 4)
                    pe.wait_ge(s_small[7], 16)
                    for t in range(TT):
                        for k in range(KC):
                            last = mm(ps[:, 0, t * NE:(t + 1) * NE], h2T[:, k, t * P:(t + 1) * P], rw[:, k, :],
                                      start=(k == 0), stop=(k == KC - 1))
                    last.then_inc(s["lg_done"], 1)
                    pe.wait_ge(s["lg_ready"], 1)
                    mm(ps[:, 1, 0:NE], upper[:, :], mask[:, 0, :], start=True, stop=True)
                    mm(ps[:, 1, NE:2 * NE], upper[:, :], mask[:, 1, :], start=True, stop=False)
                    mm(ps[:, 1, NE:2 * NE], ones[:, :], mask[:, 0, :], start=False, stop=True)
                    for t in range(TT):
                        last = mm(ps[:, 1, 2 * NE:3 * NE], ones[:, :], mask[:, t, :], start=(t == 0), stop=(t == 1))
                    last.then_inc(s["rank_done"], 1)
                    pe.wait_ge(s["rank_ready"], 2)

                    def gather(c, e, k):
                        src = (h2_hi, h2_lo)[k]
                        for f in range(KC):
                            for t in range(TT):
                                last = mm(two(6)[:, f * P:(f + 1) * P], src[:, t, f * P:(f + 1) * P],
                                          sel[:, t, :], start=(t == 0), stop=(t == TT - 1))
                        last.then_inc(s["gat_done"], 1)

                    def scatter(t):
                        for b in range(2):
                            sl, cs = slice(t * P, (t + 1) * P), slice(b * 512, (b + 1) * 512)
                            mm(ps[:, 6 + b, :], selT[:, sl], y_hi[:, cs], start=True, stop=False)
                            last = mm(ps[:, 6 + b, :], selT[:, sl], y_lo[:, cs], start=False, stop=True)
                        last.then_inc(s["sct_done"], 1)

                    def experts(base, r):
                        pe.wait_ge(s["sel_ready"], 18 * r + 2)
                        gather(18 * r, None, 0)
                        pe.wait_ge(s["gat_hi"], 18 * r + 1)
                        gather(18 * r, None, 1)
                        with pe.Fori(0, NE) as e:
                            def halves(c):
                                return At(8 + 16 * r + c, e, 2).count()

                            def pairs(c):
                                return At(18 * r + c, e, 2).count()

                            pe.wait_ge(s["gat_hi"], pairs(2))
                            for j in range(4 * KC):
                                wi, hf, k = (j // KC) % 2, j // (2 * KC), j % KC
                                if j == 4:
                                    if True:
                                        pe.wait_ge(s["ey_lo"], At(8 * r, e, 1).count()) if r else None
                                    scatter(0)
                                if j == 8:
                                    pe.wait_ge(s["sct_used"], pairs(1))
                                    scatter(1)
                                if j == 12:
                                    pe.wait_ge(s["sct_used"], pairs(2))
                                    for t in range(TT):
                                        last = mm(ps[:, 6, t * P:(t + 1) * P], sel[:, t, :], ident_r[:, :],
                                                  start=True, stop=True)
                                    last.then_inc(s["selT_done"], 1)
                                if j == 16:
                                    pe.wait_ge(s["h1_used"], halves(1))
                                if j == 20:
                                    pe.wait_ge(s["selT_used"], At(8 * r + 1, e, 1).count())
                                    pe.wait_ge(s["h3_used"], halves(1))
                                    transposes(two(6), ehid[:, 0:HC], EC // 2).then_inc(s["hT_done"], 1)
                                whs, wls = tile(At(base + j, e, N_EXP), HC)
                                for b in range(2):
                                    cs = slice(b * HC // 2, (b + 1) * HC // 2)
                                    last = prod(ps[:, 2 * wi + b, 0:HC // 2], gT_hi[:, k, :], gT_lo[:, k, :],
                                                whs[:, cs], wls[:, cs], k == 0, k == KC - 1)
                                last.then_inc(w_used, 1)
                            pe.wait_ge(s["sel_ready"], pairs(4))
                            pe.wait_ge(s["hT_lo"], halves(1))
                            gather(0, e, 0)
                            j = 4 * KC
                            for k in range(EC):
                                if k == 3:
                                    pe.wait_ge(s["gat_hi"], pairs(3))
                                    pe.wait_ge(s["h3_used"], halves(2))
                                    transposes(two(6), ehid[:, HC:FE], EC // 2).then_inc(s["hT_done"], 1)
                                if k == EC // 2:
                                    pe.wait_ge(s["hT_lo"], halves(2))
                                if k == 10:
                                    gather(0, e, 1)
                                for b in range(2):
                                    halved = k >= EC - 2
                                    T_ = At(base + j, e, N_EXP)
                                    if b == 0 or halved:
                                        whs, wls = tile(T_, D if not halved else D // 2)
                                    cs = slice(0, 512) if halved else slice(b * 512, (b + 1) * 512)
                                    last = prod(ps[:, 4 + b, :], eT_hi[:, k, :], eT_lo[:, k, :],
                                                whs[:, cs], wls[:, cs], k == 0, k == EC - 1)
                                    if b == 1 or halved:
                                        last.then_inc(w_used, 1)
                                        j += 1
                            assert j == N_EXP
                            pe.wait_ge(s["ey_lo"], At(8 * r + 1, e, 1).count())
                        pe.wait_ge(s["gat_hi"], 18 * (r + 1))
                        scatter(0)
                        pe.wait_ge(s["sct_used"], 18 * r + 2 * NE + 1)
                        scatter(1)

                    experts(MOE, 0)
                    over = pe.value_load(flag[0:1, 0:1], min_val=0, max_val=1)
                    with pe.If(over):
                        experts(OVER, 1)


_INS = ["x", "positions", "mix_norm", "w_in", "gate_bias", "conv_w", "a_log", "dt_bias", "gdn_out_norm", "w_gdn_o",
        "q_a_norm", "w_q_b", "kv_a_norm", "w_kv_b", "w_mla_o", "w_out", "ffn_norm", "dense_w1", "dense_w3",
        "dense_w2", "router_w", "moe_w1", "moe_w3", "moe_w2", "final_norm"]


def kernel(**inputs):
    import numpy as _np
    import concourse.bacc as _bacc
    from concourse import mybir as _mybir
    from concourse.bass_utils import run_bass_kernel_spmd as _run

    nc = _bacc.Bacc("TRN2", target_bir_lowering=False, num_devices=1)
    arrays, args = {}, {}
    for name in _INS:
        a = _np.ascontiguousarray(inputs[name])
        arrays[f"in_{name}"] = a
        args[name] = nc.dram_tensor(f"in_{name}", a.shape, _mybir.dt.from_np(a.dtype), kind="ExternalInput").ap()
    shape = inputs["x"].shape
    out = nc.dram_tensor("out_0", shape, _mybir.dt.float32, kind="ExternalOutput").ap()
    program(nc, args, out)
    r = _run(nc, [arrays], core_ids=[0])
    return r.results[0]["out_0"]
```

```python
from contextlib import ExitStack

import numpy as np

import concourse.bass as bass
from concourse import mybir

F32 = mybir.dt.float32
F32R = mybir.dt.float32r
I32 = mybir.dt.int32
U32 = mybir.dt.uint32
ALU = mybir.AluOpType
ACT = mybir.ActivationFunctionType
AX_X = mybir.AxisListType.X

P = 128
RAW = 8
SPL = 4
SLOT = 1024
EPS = 1e-6
BIG = 1e30
CHUNK = 64
TOP_K = 2
ROPE_THETA = 10000.0


class At:

    def __init__(self, c, i=None, per=0):
        self.c, self.i, self.per = c, i, per

    def count(self, k=0):
        return self.c + k if self.i is None else self.i * self.per + (self.c + k)

    def plus(self, k):
        return At(self.c + k, self.i, self.per)

    def landed(self):
        full = 16 * (self.c // RAW + 1)
        return full if self.i is None else self.i * (16 * self.per // RAW) + full


class Chain:

    def __init__(self, eng, sem):
        self.eng, self.sem, self.n, self.i, self.per = eng, sem, 0, None, 0

    def mark(self, ins):
        ins.then_inc(self.sem, 1)
        self.n += 1
        return At(self.n, self.i, self.per).count()

    def wait(self, value):
        self.eng.wait_ge(self.sem, value)

    def link(self, ins):
        self.wait(self.mark(ins))

    def enter(self, i, per):
        self.i, self.per, self.at = i, per, self.n

    def leave(self, times):
        assert self.n - self.at == self.per, (self.n - self.at, self.per)
        self.n = self.at + times * self.per
        self.i = None


def program(nc, A, out):
    _, T, D = A["x"].shape
    L, _, IN = A["w_in"].shape
    TT = T // P
    KC = D // P
    H = A["a_log"].shape[1]
    DV = A["gdn_out_norm"].shape[1]
    QW = H * DV
    NQK = 3 * QW // P
    QL, KVL = A["w_q_b"].shape[1], A["w_kv_b"].shape[1]
    GB = A["gate_bias"].shape[1]
    ROPE = IN - 4 * QW - 2 * H - QL - KVL - GB
    MV = A["w_mla_o"].shape[1]
    QN = A["w_q_b"].shape[2]
    KVN = A["w_kv_b"].shape[2]
    HM = (QN + MV - KVN) // ROPE
    DQ = QN // HM
    NOPE = DQ - ROPE
    VD = MV // HM
    HALF = ROPE // 2
    CONV = A["conv_w"].shape[1]
    FF = A["dense_w1"].shape[2]
    NE, FE = A["moe_w1"].shape[1], A["moe_w1"].shape[3]
    LC = (QL + KVL) // P
    QC = QL // P
    assert T == 256 and D == 1024 and H * P == 512 and DV == P and L == 2 and DQ == 96 and HM == 8
    OFF_Z, OFF_A = 3 * QW, 4 * QW
    OFF_C = OFF_A + 2 * H
    OFF_G = OFF_C + QL + KVL + ROPE
    G1 = OFF_G - OFF_A
    SUB = 448
    HC = FE // 2

    MIX = [("g1", KC), ("z", KC), ("wkv", LC - QC), ("wq", QC), ("qkv", 2 * KC),
           ("gate", 2 * KC), ("mla_o", MV // P), ("gdn_o", QW // P), ("out", KC)]
    first, at = {}, 0
    for name, n in MIX:
        first[name] = at
        at += n
    N_MIX = at
    N_UP = 16
    UPS = FF // (2 * SUB)
    N_DOWN = FF // P
    MIX0, DENSE = 0, N_MIX
    MIX1 = DENSE + UPS * N_UP + N_DOWN
    MOE = MIX1 + N_MIX
    N_EXP = 48
    EC = FE // P
    assert N_UP % RAW == 0 and N_EXP % RAW == 0 and N_UP % SPL == 0 and N_EXP % SPL == 0
    OVER = MOE + NE * N_EXP

    st = ExitStack()
    with st:
        def sb(name, shape, dt=F32, ctx=st):
            return ctx.enter_context(nc.sbuf_tensor(name, shape, dt))

        def sem(name):
            return st.enter_context(nc.semaphore(name))

        raw = sb("raw", [P, RAW, SLOT])
        whi = sb("whi", [P, SPL, SLOT], F32R)
        wlo = sb("wlo", [P, SPL, SLOT], F32R)
        x = sb("x", [P, TT, D])
        hbuf = sb("hbuf", [P, TT, D])
        aT_hi = sb("aT_hi", [P, KC, T], F32R)
        aT_lo = sb("aT_lo", [P, KC, T], F32R)
        rows = sb("rows", [P, 2, D])
        ident = sb("ident", [P, P])
        ident_r = sb("ident_r", [P, P], F32R)
        ones = sb("ones", [P, P])
        incl = sb("incl", [P, P])
        same = sb("same", [P, P])
        upper = sb("upper", [P, P])
        neg_q = sb("neg_q", [P, P])
        neg_k = sb("neg_k", [P, P])
        NLEV = 6
        lev = sb("lev", [P, NLEV, P])
        lev0 = sb("lev0", [P, P])
        slot_no = sb("slot_no", [P, 2, P])
        inchunk = sb("inchunk", [P, 2])
        ids_i = sb("ids_i", [P, P], I32)
        col_i = sb("col_i", [P, 1], I32)
        row_f = sb("row_f", [P, P])
        col_f = sb("col_f", [P, NLEV + 1])
        lv_i = sb("lv_i", [P, NLEV], I32)
        singles = sb("singles", [P, 16])
        epsc, tick = singles[:, 0:1], singles[:, 1:2]
        mhalf = singles[:, 8:16]
        ss = sb("ss", [P, TT])
        rinv = sb("rinv", [P, TT])
        posi = sb("posi", [P, TT], I32)
        ang = sb("ang", [P, 6, TT, HALF])
        cosb = sb("cosb", [P, TT, HALF])
        sinb = sb("sinb", [P, TT, HALF])

        cw_in = sb("cw_in", [CONV * NQK, L, P])
        cw = sb("cw", [P, L, CONV, NQK])
        adt = sb("adt", [P, L, 2, H])
        mix = ExitStack()
        gates = sb("gates", [P, TT, GB], F32, mix)
        pad = gates[:, :, :].rearrange("p a b -> p (a b)")[:, 0:NQK * (T + 4)].rearrange(
            "p (c t) -> p c t", c=NQK)
        PADW = 4
        zs = sb("zs", [P, TT, QW], F32, mix)
        pT_hi = sb("pT_hi", [P, LC, T], F32R, mix)
        pT_lo = sb("pT_lo", [P, LC, T], F32R, mix)
        oT_hi = sb("oT_hi", [P, MV // P, T], F32R, mix)
        oT_lo = sb("oT_lo", [P, MV // P, T], F32R, mix)
        lat_w = sb("lat_w", [P, QL + KVL], F32, mix)
        onorm = sb("onorm", [P, DV], F32, mix)
        abr = sb("abr", [P, TT, 2 * H], F32, mix)
        sp = sb("sp", [P, 6, TT, H], F32, mix)
        gl = sb("gl", [P, TT, H], F32, mix)
        beta = sb("beta", [P, TT, H], F32, mix)
        krr = sb("krr", [P, TT, ROPE], F32, mix)
        lss = sb("lss", [P, TT, 2], F32, mix)
        lri = sb("lri", [P, TT, 2], F32, mix)
        tmp_r = sb("tmp_r", [P, 2, HM, HALF], F32, mix)
        mx = sb("mx", [P, 3, HM], F32, mix)
        rs = sb("rs", [P, 3, HM], F32, mix)
        ri = sb("ri", [P, 3, HM], F32, mix)
        sums = sb("sums", [P, 64], F32, mix)
        gcol = sb("gcol", [P, 10, TT, H], F32, mix)
        cdb = sb("cdb", [P, 4, H], F32, mix)
        oss = sb("oss", [P, TT, H], F32, mix)
        ori = sb("ori", [P, TT, H], F32, mix)
        mla = ExitStack()
        qT = sb("qT", [DQ, HM, T], F32, mla)
        kT = sb("kT", [DQ, HM, T], F32, mla)
        vm = sb("vm", [P, TT, MV], F32, mla)
        om = sb("om", [P, TT, MV], F32, mla)
        stage1 = ExitStack()
        lat = sb("lat", [P, TT, QL + KVL], F32, stage1)
        qm = sb("qm", [P, TT, HM, DQ], F32, stage1)
        km = sb("km", [P, TT, HM, DQ], F32, stage1)
        stage1.close()
        stage2 = ExitStack()
        prob = sb("prob", [P, 2, D], F32, stage2)
        probT = sb("probT", [P, 2, D], F32, stage2)
        stage2.close()
        mla.close()
        gdn = ExitStack()
        qkv = sb("qkv", [P, NQK, T], F32, gdn)
        wTb = qkv[:, 0:4, :]
        ub = qkv[:, 4:8, :].rearrange("p a b -> p (a b)").rearrange("p (t n) -> p t n", t=TT)
        vnb = qkv[:, 8:12, :].rearrange("p a b -> p (a b)").rearrange("p (t n) -> p t n", t=TT)
        kb = sb("kb", [P, TT, QW], F32, gdn)
        kd = sb("kd", [P, TT, QW], F32, gdn)
        vb = sb("vb", [P, TT, QW], F32, gdn)
        Lm = sb("Lm", [P, TT, QW], F32, gdn)
        LT = sb("LT", [P, TT, QW], F32, gdn)
        X = sb("X", [P, TT, QW], F32, gdn)
        XT = sb("XT", [P, TT, QW], F32, gdn)
        MT = sb("MT", [P, TT, QW], F32, gdn)
        S = sb("S", [P, 2, QW], F32, gdn)
        gdn.close()
        mix.close()
        hflat = hbuf[:, :, :].rearrange("p a b -> p (a b)")
        inT = hflat[:, 0:TT * QW].rearrange("p (t n) -> p t n", t=TT)
        qdT = hflat[:, TT * QW:2 * TT * QW].rearrange("p (h t) -> p h t", h=H)

        dns = ExitStack()
        dT_hi = sb("dT_hi", [P, N_DOWN, T], F32R, dns)
        dT_lo = sb("dT_lo", [P, N_DOWN, T], F32R, dns)
        dhid = sb("dhid", [P, TT, 2 * SUB], F32, dns)
        dsil = sb("dsil", [P, 2, TT, SUB], F32, dns)
        dns.close()
        moe = ExitStack()
        h2_hi = sb("h2_hi", [P, TT, D], F32R, moe)
        h2_lo = sb("h2_lo", [P, TT, D], F32R, moe)
        h2T = sb("h2T", [P, KC, T], F32, moe)
        rw = sb("rw", [P, KC, NE], F32, moe)
        gT_hi = sb("gT_hi", [P, KC, P], F32R, moe)
        gT_lo = sb("gT_lo", [P, KC, P], F32R, moe)
        ehid = sb("ehid", [P, FE], F32, moe)
        esil = sb("esil", [P, HC], F32, moe)
        eT_hi = sb("eT_hi", [P, EC, P], F32R, moe)
        eT_lo = sb("eT_lo", [P, EC, P], F32R, moe)
        y_hi = sb("y_hi", [P, D], F32R, moe)
        y_lo = sb("y_lo", [P, D], F32R, moe)
        sel = sb("sel", [P, TT, P], F32R, moe)
        selT = sb("selT", [P, T], F32R, moe)
        lg = sb("lg", [P, TT, NE], F32, moe)
        top = sb("top", [P, TT, 8], F32, moe)
        topi = sb("topi", [P, TT, 8], U32, moe)
        topf = sb("topf", [P, TT, 2], F32, moe)
        tw = sb("tw", [P, TT, 4], F32, moe)
        oneh = sb("oneh", [P, 2, TT, NE], F32, moe)
        mask = sb("mask", [P, TT, NE], F32, moe)
        comb = sb("comb", [P, TT, NE + 1], F32, moe)
        rank = sb("rank", [P, TT, NE + 1], F32, moe)
        cmax = sb("cmax", [P, 2], F32, moe)
        flag = sb("flag", [P, 1], I32, moe)
        moe.close()

        ps = st.enter_context(nc.psum_tensor("ps", [P, 8, 512], F32))

        def two(b):
            return ps[:, b:b + 2, :].rearrange("p a b -> p (a b)")

        s_raw = [sem(f"s_raw{i}") for i in range(RAW)]
        w_hi = sem("w_hi")
        w_lo = sem("w_lo")
        w_used = sem("w_used")
        s_x = sem("s_x")
        s_small = [sem(f"s_small{i}") for i in range(8)]
        s_row = [sem("s_row0"), sem("s_row1")]
        row_used = sem("row_used")
        s_out = sem("s_out")
        chain_v, chain_a, chain_p = sem("chain_v"), sem("chain_a"), sem("chain_p")
        names = """ids consts ident_ready norm_ss norm_r norm_h norm_T norm_hi norm_lo cwT cw_ready
            z_ready lat_ss lat_r lat_h lat_T lat_hi lat_lo g1_used g_ready
            q_copied q_rope kv_copied k_rope qk_T qk_Tc sc_done sc_masked sc_exp
            p_T p_Tc pv_done o_norm om_T om_hi om_lo pad_ready tap0 conv_done qkv_ready
            sq_ready sums_done sums_used lnrow lncols cols_ready row_done row_exp
            eq_in e_exp kk_done L_ready LT_done LT_ready kt_done kt_used inv_ready
            y_done y_ready zz_done x_ready w_done w_ready u_ready v_done vn_ready o_done s_done
            s_ready o_ss o_r og_ready og_T og_hi og_lo gate_in gate_ready
            oa_in gdn_half merged m_T m_hi m_lo out_half x_new
            down_half h1_used h3_used hT_done hT_hi hT_lo
            sel_in lg_done lg_ready e_ready rank_done rank_ready sel_ready selT_done
            selT_used gat_done gat_hi
            ey_hi ey_lo sct_done sct_used over_done trig""".split()
        s = {n: sem(n) for n in names}

        block = st.enter_context(nc.Block())

        def src2(w, rows0, c0, c1):
            return w[rows0:rows0 + P, c0:c1]

        def mix_tiles(l):
            w = A["w_in"][l]
            o = [src2(w, k * P, OFF_A, OFF_G) for k in range(KC)]
            o += [src2(w, k * P, OFF_Z, OFF_A) for k in range(KC)]
            o += [src2(A["w_kv_b"][l], k * P, 0, KVN) for k in range(LC - QC)]
            o += [src2(A["w_q_b"][l], k * P, 0, QN) for k in range(QC)]
            for hf in range(2):
                o += [src2(w, k * P, hf * 3 * QW // 2, (hf + 1) * 3 * QW // 2) for k in range(KC)]
            for hf in range(2):
                o += [src2(w, k * P, OFF_G + hf * D, OFF_G + (hf + 1) * D) for k in range(KC)]
            o += [src2(A["w_mla_o"][l], k * P, 0, D) for k in range(MV // P)]
            o += [src2(A["w_gdn_o"][l], k * P, 0, D) for k in range(QW // P)]
            o += [src2(A["w_out"][l], k * P, 0, D) for k in range(KC)]
            return o

        MIX_COLS = [v.shape[1] for v in mix_tiles(0)]
        EXP_COLS = [HC] * (4 * KC) + [D] * (EC - 2) + [D // 2] * 4

        @block.sync
        def _(sync):
            def load(t, dst, src):
                if t.c >= RAW:
                    sync.wait_ge(w_lo, t.count(1 - RAW))
                sync.dma_start(dst, src).then_inc(s_raw[t.c % RAW], 16)

            def slot(t, n):
                return raw[:, t.c % RAW, 0:n]

            def mixer(l, base):
                for j, src in enumerate(mix_tiles(l)):
                    t = At(base + j)
                    load(t, slot(t, src.shape[1]), src)

            sync.dma_start(x[:, :, :], A["x"][0].rearrange("(t p) d -> p t d", p=P)).then_inc(s_x, 16)
            mixer(0, MIX0)
            with sync.Fori(0, UPS) as i:
                for sub in range(2):
                    for wi, w in enumerate((A["dense_w1"][0], A["dense_w3"][0])):
                        for k in range(4):
                            t = At(DENSE + sub * 8 + wi * 4 + k, i, N_UP)
                            src = w[2 * P * k:2 * P * (k + 1), bass.ds(i * (2 * SUB) + sub * SUB, SUB)]
                            load(t, slot(t, 2 * SUB).rearrange("p (a n) -> p a n", a=2),
                                 src.rearrange("(a p) n -> p a n", p=P))
            for k in range(N_DOWN):
                t = At(DENSE + UPS * N_UP + k)
                load(t, slot(t, D), src2(A["dense_w2"][0], k * P, 0, D))
            mixer(1, MIX1)

            def experts(base):
                w1 = A["moe_w1"][0].rearrange("e d f -> (e d) f")
                w3 = A["moe_w3"][0].rearrange("e d f -> (e d) f")
                w2 = A["moe_w2"][0].rearrange("e f d -> (e f) d")
                with sync.Fori(0, NE) as e:
                    j = 0
                    for hf in range(2):
                        for w in (w1, w3):
                            for k in range(KC):
                                t = At(base + j, e, N_EXP)
                                load(t, slot(t, HC), w[bass.ds(e * D + k * P, P), hf * HC:(hf + 1) * HC])
                                j += 1
                    for k in range(EC):
                        for c in ([0] if k < EC - 2 else [0, 1]):
                            n = EXP_COLS[j]
                            t = At(base + j, e, N_EXP)
                            load(t, slot(t, n), w2[bass.ds(e * FE + k * P, P), c * n:(c + 1) * n])
                            j += 1
                    assert j == N_EXP

            experts(MOE)
            sync.wait_ge(s["rank_ready"], 2)
            over = sync.value_load(flag[0:1, 0:1], min_val=0, max_val=1)
            with sync.If(over):
                experts(OVER)
            sync.wait_ge(s["norm_h"], 2 * 5)
            sync.dma_start(out[0].rearrange("(t p) d -> p t d", p=P), hbuf[:, :, :]).then_inc(s_out, 16)
            sync.wait_ge(s_out, 16)

        @block.gpsimd
        def _(pool):
            ch = Chain(pool, chain_p)
            pool.iota(ids_i[:, :], pattern=[[1, P]], base=0, channel_multiplier=0).then_inc(s["ids"], 1)
            pool.iota(col_i[:, :], pattern=[[0, 1]], base=0, channel_multiplier=1).then_inc(s["ids"], 1)
            pool.memset(mhalf[:, :], -0.5).then_inc(s["ids"], 1)
            pool.memset(ones[:, :], 1.0).then_inc(s["ids"], 1)
            pool.memset(epsc[:, :], EPS).then_inc(s["ids"], 1)
            pool.wait_ge(s["ids"], 5)
            seq = []
            for l in range(L):
                seq += [A["mix_norm"][l], A["gate_bias"][l, 0:D], A["gate_bias"][l, D:2 * D], A["ffn_norm"][l]]
            seq.append(A["final_norm"][:])

            def row(r):
                if r >= 2:
                    pool.wait_ge(row_used, r - 1)
                pool.dma_start(rows[:, r % 2, :], seq[r].rearrange("(a d) -> a d", a=1).to_broadcast([P, D])
                               ).then_inc(s_row[r % 2], 16)

            def small(i, dst, src):
                pool.dma_start(dst, src).then_inc(s_small[i], 16)

            def bc(v, n):
                return v.rearrange("(a d) -> a d", a=1).to_broadcast([P, n])

            row(0)
            with nc.allow_non_contiguous_dma(reason="256 positions"):
                small(0, posi[:, :], A["positions"][0].rearrange("(t p) -> p t", p=P))
            small(1, cw_in[:, :, :], A["conv_w"].rearrange("l k (c p) -> (k c) l p", p=P) if False else
                  A["conv_w"].rearrange("l k (c p) -> l (k c) p", p=P).rearrange("l a p -> a l p"))
            small(2, adt[:, :, 0, :], A["a_log"].rearrange("(o l) h -> o l h", o=1).to_broadcast([P, L, H]))
            small(3, adt[:, :, 1, :], A["dt_bias"].rearrange("(o l) h -> o l h", o=1).to_broadcast([P, L, H]))

            def rms(dst, src):
                w = mhalf[:, 0:src.shape[1]] if len(src.shape) == 2 else \
                    mhalf[:, 0:TT * H].rearrange("p (a b) -> p a b", a=TT)
                ch.link(pool.tensor_scalar(dst, src, EPS, None, ALU.add))
                return pool.tensor_tensor(dst, dst, w, ALU.pow)

            def norm(n):
                for t in range(TT):
                    pool.wait_ge(s["norm_ss"], TT * n + t + 1)
                    rms(rinv[:, t:t + 1], ss[:, t:t + 1]).then_inc(s["norm_r"], 1)

            def masks():
                pool.wait_ge(s["ident_ready"], 2)
                pts, ptt, cp, lk = pool.tensor_scalar, pool.tensor_tensor, pool.tensor_copy, ch.link
                for r in range(2):
                    lk(pts(slot_no[:, r, :], row_f[:, :], float(1 + r * P), None, ALU.add))
                lk(pts(upper[:, :], row_f[:, :], col_f[:, 0:1], None, ALU.is_gt))
                lk(pts(neg_q[:, :], row_f[:, :], col_f[:, 0:1], None, ALU.is_lt))
                lk(cp(same[:, :], ident[:, :]))
                for k in range(NLEV):
                    lk(pool.iota(ids_i[:, :], pattern=[[1, P >> (k + 1)], [0, 2 << k]], base=0, channel_multiplier=0))
                    lk(cp(row_f[:, :], ids_i[:, :]))
                    lk(pts(row_f[:, :], row_f[:, :], col_f[:, k + 1:k + 2], None, ALU.is_equal))
                    lk(ptt(lev[:, k, :], row_f[:, :], same[:, :], ALU.subtract))
                    lk(cp(same[:, :], row_f[:, :]))
                lk(ptt(lev0[:, :], lev[:, 0, :], neg_q[:, :], ALU.mult))
                for k in range(NLEV):
                    lk(ptt(lev[:, k, :], lev[:, k, :], upper[:, :], ALU.mult))
                lk(pts(inchunk[:, 1:2], col_f[:, NLEV:NLEV + 1], 1.0, None, ALU.mult))
                lk(pts(inchunk[:, 0:1], col_f[:, NLEV:NLEV + 1], -1.0, 1.0, ALU.mult, ALU.add))
                lk(ptt(neg_k[:, :], neg_q[:, :], same[:, :], ALU.mult))
                lk(pts(neg_k[:, :], neg_k[:, :], -BIG, BIG, ALU.mult, ALU.add))
                lk(pts(neg_q[:, :], neg_q[:, :], -1.0, 1.0, ALU.mult, ALU.add))
                lk(ptt(incl[:, :], neg_q[:, :], same[:, :], ALU.mult))
                pts(neg_q[:, :], incl[:, :], BIG, -BIG, ALU.mult, ALU.add).then_inc(s["consts"], 1)

            for l in range(L):
                small(4, lat_w[:, 0:QL], bc(A["q_a_norm"][l], QL))
                small(5, lat_w[:, QL:QL + KVL], bc(A["kv_a_norm"][l], KVL))
                small(6, onorm[:, :], bc(A["gdn_out_norm"][l], DV))
                norm(2 * l)
                row(4 * l + 1)
                for t in range(TT):
                    pool.wait_ge(s["lat_ss"], 4 * l + 2 * (t + 1))
                    rms(lri[:, t, :], lss[:, t, :]).then_inc(s["lat_r"], 1)
                if l == 0:
                    masks()
                row(4 * l + 2)
                for t in range(TT):
                    pool.wait_ge(s["o_ss"], H * (TT * l + t + 1))
                    rms(ori[:, t, :], oss[:, t, :]).then_inc(s["o_r"], 1)
                row(4 * l + 3)
                norm(2 * l + 1)
                row(4 * l + 4)
                if l == 0:
                    pool.wait_ge(s["x_new"], 2 * TT)
            with nc.allow_non_contiguous_dma(reason="rows of 8 router weights"):
                small(7, rw[:, :, :], A["router_w"][0].rearrange("(k p) e -> p k e", p=P))
            pool.wait_ge(s["rank_ready"], 2)
            norm(2 * L)
            pool.wait_ge(s_small[7], 16)

        @block.scalar
        def _(act):
            ch = Chain(act, chain_a)
            a = nc.scalar.activation
            done = [0]

            def split(t, n):
                act.wait_ge(s_raw[t.c % RAW], t.landed())
                if t.c >= SPL:
                    act.wait_ge(w_used, t.count(1 - SPL))
                a(whi[:, t.c % SPL, 0:n], raw[:, t.c % RAW, 0:n], ACT.Copy).then_inc(w_hi, 1)

            def upto(base, n):
                while done[0] < min(base + n, base + N_MIX):
                    split(At(done[0]), MIX_COLS[done[0] - base])
                    done[0] += 1

            def norm(n, ahead=None, split_T=True):
                for t in range(TT):
                    if 1 <= n <= 3:
                        act.wait_ge(s["x_new"], TT * (n - 1) + t + 1)
                    a(hbuf[:, t, :], x[:, t, :], ACT.Square, scale=float(D) ** -0.5,
                      accum_out=ss[:, t:t + 1]).then_inc(s["norm_ss"], 1)
                    if ahead:
                        ahead(t)
                if n == 2 * L:
                    return
                if ahead:
                    ahead(TT)
                for t in range(TT):
                    act.wait_ge(s["norm_T"], TT * n + t + 1)
                    src = two(4 + 2 * t).rearrange("p (k n) -> p k n", k=KC)
                    if split_T:
                        a(aT_hi[:, :, t * P:(t + 1) * P], src, ACT.Copy).then_inc(s["norm_hi"], 1)
                    else:
                        a(h2T[:, :, t * P:(t + 1) * P], src, ACT.Copy).then_inc(s["norm_hi"], 1)

            act.wait_ge(s_x, 16)

            for l in range(L):
                base = (MIX0, MIX1)[l]
                done[0] = base
                norm(2 * l, lambda k: upto(base, k + 1))
                upto(base, 4)
                if l == 0:
                    act.wait_ge(s["trig"], 1)
                    a(sinb[:, :, :], ang[:, 0, :, :], ACT.Sin).then_inc(s["trig"], 1)
                    a(cosb[:, :, :], ang[:, 1, :, :], ACT.Sin).then_inc(s["trig"], 1)
                upto(base, first["z"] + SPL - 1)
                act.wait_ge(w_used, base + first["z"])
                for t in range(TT):
                    v = two(2 * t)[:, 2 * H:2 * H + QL + KVL]
                    for j, (c0, c1) in enumerate(((0, QL), (QL, QL + KVL))):
                        a(om[:, t, c0:c1] if j == 0 else vm[:, t, 0:KVL], v[:, c0:c1], ACT.Square,
                          scale=float(c1 - c0) ** -0.5, accum_out=lss[:, t, j:j + 1]).then_inc(s["lat_ss"], 1)
                    v = two(2 * t)[:, 0:G1]
                    a(abr[:, t, :], v[:, 0:2 * H], ACT.Copy).then_inc(s["g1_used"], 1)
                    a(krr[:, t, :], v[:, G1 - ROPE:G1], ACT.Copy).then_inc(s["g1_used"], 1)
                if l == 0:
                    act.wait_ge(s["cwT"], L)
                    for i in range(L):
                        a(cw[:, i, :, :], ps[:, 6 + i, 0:CONV * NQK].rearrange("p (k c) -> p k c", k=CONV),
                          ACT.Copy).then_inc(s["cw_ready"], 1)
                upto(base, first["wkv"])
                for t in range(TT):
                    act.wait_ge(s["lat_T"], TT * l + t + 1)
                    a(pT_hi[:, :, t * P:(t + 1) * P], two(6 - 6 * t)[:, 0:LC * P].rearrange("p (k n) -> p k n", k=LC),
                      ACT.Copy).then_inc(s["lat_hi"], 1)
                upto(base, first["wkv"] + 2)
                act.wait_ge(w_used, base + first["wkv"])
                for t in range(TT):
                    a(zs[:, t, :], ps[:, 4 + t, :], ACT.Silu).then_inc(s["z_ready"], 1)
                upto(base, first["wq"] + 2)
                act.wait_ge(w_used, base + first["wq"])
                for t in range(TT):
                    v = two(2 * t)[:, 0:KVN].rearrange("p (h d) -> p h d", h=HM)
                    a(km[:, t, :, 0:NOPE], v[:, :, 0:NOPE], ACT.Copy).then_inc(s["kv_copied"], 1)
                    a(vm[:, t, :].rearrange("p (h d) -> p h d", h=HM), v[:, :, NOPE:NOPE + VD],
                      ACT.Copy).then_inc(s["kv_copied"], 1)
                upto(base, first["qkv"] + 2)
                act.wait_ge(w_used, base + first["qkv"])
                for t in range(TT):
                    a(qm[:, t, :, :], two(4 + 2 * t)[:, 0:QN].rearrange("p (h d) -> p h d", h=HM),
                      ACT.Copy).then_inc(s["q_copied"], 1)
                for u in range(4):
                    upto(base, first["qkv"] + 4 + 2 * (u // 2) + 2)
                    act.wait_ge(s["qk_T"], 4 * l + u + 1)
                    dst = (qT, kT)[u // 2]
                    a(dst[:, :, (u % 2) * P:(u % 2 + 1) * P],
                      two(4 + 2 * (u % 2))[0:DQ, :].rearrange("p (h n) -> p h n", h=HM),
                      ACT.Copy).then_inc(s["qk_Tc"], 1)

                def evac_qkv(hf):
                    act.wait_ge(w_used, base + first["qkv"] + KC * (hf + 1))
                    n = NQK // 2
                    a(pad[:, hf * n:(hf + 1) * n, 3:3 + T],
                      ps[:, 0:3, :].rearrange("p a (b t) -> p (a b) t", b=2), ACT.Copy).then_inc(s["pad_ready"], 1)

                def exps(u):
                    nh, nk = (HM, P) if u == 0 else (HM // 2, T)
                    act.wait_ge(s["sc_masked"], 3 * l + u + 1)
                    if u == 2:
                        act.wait_ge(s["p_T"], 3 * l + 1)
                    for h in range(nh):
                        a(prob[:, u % 2, h * nk:(h + 1) * nk], two(3)[:, h * nk:(h + 1) * nk], ACT.Exp,
                          bias=mx[:, u, h:h + 1], scale=float(DQ) ** -0.5,
                          accum_out=rs[:, u, h:h + 1]).then_inc(s["sc_exp"], 1)

                def probs_T(u):
                    act.wait_ge(s["p_T"], 3 * l + u + 1)
                    if u == 2:
                        act.wait_ge(s["pv_done"], 3 * l + 1)
                    a(probT[:, u % 2, :], two(5), ACT.Copy).then_inc(s["p_Tc"], 1)

                upto(base, first["qkv"] + 10)
                evac_qkv(0)
                exps(0)
                upto(base, first["qkv"] + 12)
                probs_T(0)
                exps(1)
                upto(base, first["qkv"] + 14)
                probs_T(1)
                exps(2)
                upto(base, first["qkv"] + 16)
                probs_T(2)
                act.wait_ge(s["g_ready"], 3 * l + 1)
                ch.mark(a(sp[:, 4, :, :], abr[:, :, H:2 * H], ACT.Exp, scale=-1.0))
                ch.mark(a(adt[:, l, 0, :], adt[:, l, 0, :], ACT.Exp))
                ch.link(a(sp[:, 2, :, :], sp[:, 1, :, :], ACT.Exp))
                evac_qkv(1)
                upto(base, first["gate"] + 3)
                for t in range(TT):
                    act.wait_ge(s["om_T"], TT * l + t + 1)
                    a(oT_hi[:, :, t * P:(t + 1) * P], ps[:, 4 + t, :].rearrange("p (k n) -> p k n", n=P),
                      ACT.Copy).then_inc(s["om_hi"], 1)
                act.wait_ge(s["pad_ready"], 3 * l + 3)
                act.wait_ge(s["om_T"], TT * (l + 1))
                act.wait_ge(s["o_norm"], 2 * (l + 1))
                for c in range(NQK):
                    a(qkv[:, c, :], pad[:, c, 0:T], ACT.Copy, scale=cw[:, l, 0, c:c + 1]).then_inc(s["tap0"], 1)
                a(sp[:, 3, :, :], sp[:, 2, :, :], ACT.Ln, bias=1.0).then_inc(s["g_ready"], 1)
                upto(base, first["gate"] + 5)
                act.wait_ge(s["conv_done"], l + 1)
                for hf in range(3):
                    v = qkv[:, hf * H:(hf + 1) * H, :]
                    a(v, v, ACT.Silu).then_inc(s["qkv_ready"], 1)
                act.wait_ge(s["qkv_ready"], 3 * (l + 1))
                sq = X[:, :, :].rearrange("p a b -> p (a b)"), XT[:, :, :].rearrange("p a b -> p (a b)")
                for j in range(2):
                    a(sq[j].rearrange("p (c t) -> p c t", c=H), qkv[:, j * H:(j + 1) * H, :],
                      ACT.Square).then_inc(s["sq_ready"], 1)
                upto(base, first["gate"] + 8)
                act.wait_ge(s["sums_used"], l + 1)
                a(gcol[:, 0:2, :, :], sums[:, 0:16].rearrange("p (j t h) -> p j t h", j=2, t=TT), ACT.Ln,
                  bias=epsc[:, 0:1]).then_inc(s["lnrow"], 1)
                act.wait_ge(s["lncols"], l + 1)
                ch.link(a(gcol[:, 7, :, :], gcol[:, 4, :, :], ACT.Exp))
                ch.link(a(cdb[:, :, :], sums[:, 32:48].rearrange("p (c h) -> p c h", c=4), ACT.Exp))
                a(gcol[:, 8, :, :], gcol[:, 6, :, :], ACT.Exp).then_inc(s["cols_ready"], 1)
                upto(base, first["gate"] + 9)
                for t in range(TT):
                    act.wait_ge(s["row_done"], TT * l + t + 1)
                    a(qdT[:, :, t * P:(t + 1) * P], ps[:, 4 + t, :].rearrange("p (h n) -> p h n", h=H),
                      ACT.Exp).then_inc(s["row_exp"], 1)
                for t in range(TT):
                    act.wait_ge(s["eq_in"], TT * l + t + 1)
                    for h in range(H):
                        hs = slice(h * P, (h + 1) * P)
                        a(inT[:, t, hs], inT[:, t, hs], ACT.Exp, bias=gcol[:, 5, t, h:h + 1]).then_inc(s["e_exp"], 1)
                        a(Lm[:, t, hs], Lm[:, t, hs], ACT.Exp, scale=-1.0,
                          bias=gcol[:, 4, t, h:h + 1]).then_inc(s["e_exp"], 1)
                upto(base, first["gate"] + 10)
                for t in range(TT):
                    act.wait_ge(s["LT_done"], TT * l + t + 1)
                    a(LT[:, t, :], ps[:, 4 + t, :], ACT.Copy).then_inc(s["LT_ready"], 1)
                for k in range(1, NLEV):
                    upto(base, first["gate"] + min(11 + k, 16))
                    for t in range(TT):
                        act.wait_ge(s["y_done"], (5 * l + k - 1) * TT + t + 1)
                        a(Lm[:, t, :], ps[:, 4 + t, :], ACT.Copy).then_inc(s["y_ready"], 1)
                    if k == 1:
                        act.wait_ge(s["gate_in"], 4 * l + 2)
                        for t in range(TT):
                            v = gates[:, t, 0:D]
                            a(v, v, ACT.Sigmoid).then_inc(s["gate_ready"], 1)
                upto(base, first["mla_o"] + 2)
                for t in range(TT):
                    act.wait_ge(s["w_done"], TT * l + t + 1)
                    a(wTb[:, :, t * P:(t + 1) * P], ps[:, 4 + t, :].rearrange("p (h n) -> p h n", h=H),
                      ACT.Copy).then_inc(s["w_ready"], 1)
                act.wait_ge(s["gate_in"], 4 * (l + 1))
                for t in range(TT):
                    v = gates[:, t, D:2 * D]
                    a(v, v, ACT.Sigmoid).then_inc(s["gate_ready"], 1)
                for t in range(TT):
                    upto(base, first["mla_o"] + 3 + 2 * t)
                    act.wait_ge(s["o_done"], 4 * l + 2 * (t + 1))
                    for h in range(H):
                        hs = slice(h * P, (h + 1) * P)
                        a(XT[:, t, hs], ps[:, 6 + t, hs], ACT.Square, scale=float(DV) ** -0.5,
                          accum_out=oss[:, t, h:h + 1]).then_inc(s["o_ss"], 1)
                for t in range(TT):
                    upto(base, first["gdn_o"] + 2 + t)
                    act.wait_ge(s["og_T"], TT * l + t + 1)
                    a(pT_hi[:, 0:H, t * P:(t + 1) * P], ps[:, 4 + t, :].rearrange("p (k n) -> p k n", n=P),
                      ACT.Copy).then_inc(s["og_hi"], 1)
                upto(base, first["out"] + 3)
                for t in range(TT):
                    act.wait_ge(s["m_T"], TT * l + t + 1)
                    a(aT_hi[:, :, t * P:(t + 1) * P], two(2 * t).rearrange("p (k n) -> p k n", k=KC),
                      ACT.Copy).then_inc(s["m_hi"], 1)
                upto(base, N_MIX)
                if l == 0:
                    norm(1, lambda k: split(At(DENSE + k), 2 * SUB))

                    def transposed(i, d):
                        for t in range(TT):
                            act.wait_ge(s["hT_done"], At(t + 1 - d * TT, i, TT).count())
                            k0 = 0 if i is None else i * 7 - 7 * d
                            a(dT_hi[:, bass.ds(k0, 7), t * P:(t + 1) * P],
                              two(4 + 2 * t)[:, 0:2 * SUB].rearrange("p (k n) -> p k n", n=P),
                              ACT.Copy).then_inc(s["hT_hi"], 1)

                    def up(i):
                        for j in range(0 if i is not None else TT + 1, N_UP):
                            split(At(DENSE + j, i, N_UP), 2 * SUB)
                            if j == 3 + SPL and i is not None:
                                transposed(i, 1)
                            if j in (7, 15):
                                act.wait_ge(w_used, At(DENSE + j - 3, i, N_UP).count())
                                sub = j // 8
                                a(dsil[:, sub, :, :], ps[:, 0:TT, 0:SUB], ACT.Silu).then_inc(s["h1_used"], 1)

                    up(None)
                    with act.Fori(1, UPS) as i:
                        up(i)
                    split(At(MIX1 - N_DOWN), D)
                    for t in range(TT):
                        act.wait_ge(s["hT_done"], TT * (UPS - 1) + t + 1)
                        a(dT_hi[:, N_DOWN - 7:N_DOWN, t * P:(t + 1) * P],
                          two(4 + 2 * t)[:, 0:2 * SUB].rearrange("p (k n) -> p k n", n=P),
                          ACT.Copy).then_inc(s["hT_hi"], 1)
                    for k in range(1, N_DOWN):
                        split(At(DENSE + UPS * N_UP + k), D)
                else:
                    norm(3, None, False)
                    for t in range(TT):
                        act.wait_ge(s["sel_in"], t + 1)
                        a(h2_hi[:, t, :], hbuf[:, t, :], ACT.Copy).then_inc(s["e_ready"], 1)
                    act.wait_ge(s["lg_ready"], 1)
                    a(tw[:, :, 1:2], tw[:, :, 0:1], ACT.Exp).then_inc(s["e_ready"], 1)

                    def gathered(e, c, k):
                        act.wait_ge(s["gat_done"], At(c + k + 1, e, 2).count())
                        dst = (gT_hi, gT_lo)[k]
                        a(dst[:, :, :], two(6).rearrange("p (k n) -> p k n", k=KC), ACT.Copy).then_inc(s["gat_hi"], 1)

                    def experts(base, r):
                        for k in range(2):
                            gathered(None, 18 * r, k)
                        with act.Fori(0, NE) as e:
                            def halves(c):
                                return At(8 + 16 * r + c, e, 2).count()

                            for j in range(N_EXP):
                                split(At(base + j, e, N_EXP), EXP_COLS[j])
                                if j in (3 + 8, 3 + 24):
                                    hf = j // 16
                                    act.wait_ge(w_used, At(base + (2 * hf + 1) * KC, e, N_EXP).count())
                                    act.wait_ge(s["h3_used"], halves(hf))
                                    a(esil[:, :].rearrange("p (a n) -> p a n", a=2), ps[:, 0:2, 0:HC // 2],
                                      ACT.Silu).then_inc(s["h1_used"], 1)
                                if j == 15:
                                    act.wait_ge(s["selT_done"], At(8 * r + 1, e, 1).count())
                                    a(selT[:, :], ps[:, 6, 0:T], ACT.Copy).then_inc(s["selT_used"], 1)
                                if j in (22, 38):
                                    hf = j // 32
                                    cs = slice(hf * EC // 2, (hf + 1) * EC // 2)
                                    act.wait_ge(s["hT_done"], halves(hf + 1))
                                    a(eT_hi[:, cs, :], two(6)[:, 0:HC].rearrange("p (k n) -> p k n", n=P),
                                      ACT.Copy).then_inc(s["hT_hi"], 1)
                                if j == 35:
                                    gathered(e, 18 * r + 2, 0)
                                if j == 45:
                                    gathered(e, 18 * r + 2, 1)
                            act.wait_ge(w_used, At(base + N_EXP, e, N_EXP).count())
                            a(y_hi[:, :], two(4), ACT.Copy).then_inc(s["ey_hi"], 1)

                    experts(MOE, 0)
                    act.wait_ge(s["rank_ready"], 2)
                    over = act.value_load(flag[0:1, 0:1], min_val=0, max_val=1)
                    with act.If(over):
                        experts(OVER, 1)
                    act.wait_ge(s["over_done"], 1)
                    norm(2 * L)

        @block.vector
        def _(dve):
            v = nc.vector
            ch = Chain(dve, chain_v)
            link, mark = ch.link, ch.mark
            done = [0]
            tt, ts, stt = v.tensor_tensor, v.tensor_scalar, v.scalar_tensor_tensor

            def split(t, n):
                dve.wait_ge(w_hi, t.count(1))
                tt(wlo[:, t.c % SPL, 0:n], raw[:, t.c % RAW, 0:n], whi[:, t.c % SPL, 0:n].bitcast(F32),
                   ALU.subtract).then_inc(w_lo, 1)

            def upto(base, n):
                while done[0] < min(base + n, base + N_MIX):
                    split(At(done[0]), MIX_COLS[done[0] - base])
                    done[0] += 1

            dve.wait_ge(s["ids"], 5)
            link(v.tensor_copy(row_f[:, :], ids_i[:, :]))
            link(v.tensor_copy(col_f[:, 0:1], col_i[:, :]))
            link(ts(ident[:, :], row_f[:, :], col_f[:, 0:1], None, ALU.is_equal))
            v.tensor_copy(ident_r[:, :], ident[:, :]).then_inc(s["ident_ready"], 1)
            for k in range(NLEV):
                mark(ts(lv_i[:, k:k + 1], col_i[:, :], k + 1, None, ALU.arith_shift_right))
            ch.wait(ch.n)
            v.tensor_copy(col_f[:, 1:NLEV + 1], lv_i[:, :]).then_inc(s["ident_ready"], 1)
            def angles():
                dve.wait_ge(s_small[0], 16)
                inv = (1.0 / (ROPE_THETA ** (np.arange(0, ROPE, 2, dtype=np.float32) / np.float32(ROPE)))).astype(np.float32)
                link(v.tensor_copy(ang[:, 2, :, 0], posi[:, :]))
                for j in range(HALF - 1, -1, -1):
                    mark(ts(ang[:, 3, :, j], ang[:, 2, :, 0], float(inv[j]), None, ALU.mult))
                ch.wait(ch.n)
                MAGIC = 1.5 * 2.0 ** 23
                C1 = 6.28125
                C2 = float(np.float32(2 * np.pi - C1).astype(np.float32))
                C2 = float(np.frombuffer(np.uint32(np.float32(C2).view(np.uint32) & 0xFFFFF000).tobytes(), np.float32)[0])
                C3 = float(np.float32(2 * np.pi - C1 - C2))
                link(ts(ang[:, 4, :, :], ang[:, 3, :, :], float(1 / (2 * np.pi)), None, ALU.mult))
                link(ts(ang[:, 4, :, :], ang[:, 4, :, :], MAGIC, None, ALU.add))
                link(ts(ang[:, 4, :, :], ang[:, 4, :, :], -MAGIC, None, ALU.add))
                for c in (C1, C2, C3):
                    link(stt(ang[:, 3, :, :], ang[:, 4, :, :], -c, ang[:, 3, :, :], ALU.mult, ALU.add))
                PI = float(np.nextafter(np.float32(np.pi), np.float32(0)))
                link(ts(ang[:, 0, :, :], ang[:, 3, :, :], PI, -PI, ALU.min, ALU.max))
                link(ts(ang[:, 5, :, :], ang[:, 3, :, :], float(np.pi / 2), None, ALU.add))
                link(ts(ang[:, 4, :, :], ang[:, 5, :, :], PI, -2 * np.pi, ALU.is_gt, ALU.mult))
                link(tt(ang[:, 5, :, :], ang[:, 5, :, :], ang[:, 4, :, :], ALU.add))
                ts(ang[:, 1, :, :], ang[:, 5, :, :], PI, -PI, ALU.min, ALU.max).then_inc(s["trig"], 1)

            def norm(n, row, ahead=None, split_T=True):
                dve.wait_ge(s_row[row % 2], 16 * (row // 2 + 1))
                for t in range(TT):
                    dve.wait_ge(s["norm_r"], TT * n + t + 1)
                    stt(hbuf[:, t, :], x[:, t, :], rinv[:, t:t + 1], rows[:, row % 2, :], ALU.mult, ALU.mult
                        ).then_inc(s["norm_h"], 1)
                    if ahead:
                        ahead(t)
                dve.wait_ge(s["norm_h"], TT * (n + 1))
                v.memset(tick[:, :], 0.0).then_inc(row_used, 1)
                if ahead:
                    ahead(TT)
                if n == 2 * L or not split_T:
                    return
                for t in range(TT):
                    dve.wait_ge(s["norm_hi"], TT * n + t + 1)
                    sl = slice(t * P, (t + 1) * P)
                    tt(aT_lo[:, :, sl], two(4 + 2 * t).rearrange("p (k n) -> p k n", k=KC),
                       aT_hi[:, :, sl].bitcast(F32), ALU.subtract).then_inc(s["norm_lo"], 1)

            def bc(ap, n):
                return ap.unsqueeze(2).to_broadcast([P, ap.shape[1], n])

            for l in range(L):
                base = (MIX0, MIX1)[l]
                done[0] = base
                norm(2 * l, 4 * l, lambda k: upto(base, k + 1))
                upto(base, 4)
                if l == 0:
                    angles()
                upto(base, first["z"] + SPL - 1)
                dve.wait_ge(s_small[4], 16 * (l + 1))
                dve.wait_ge(s_small[5], 16 * (l + 1))
                for t in range(TT):
                    dve.wait_ge(s["g1_used"], 4 * l + 2 * (t + 1))
                    dve.wait_ge(s["lat_r"], TT * l + t + 1)
                    v_ = two(2 * t)[:, 2 * H:2 * H + QL + KVL]
                    mark(stt(lat[:, t, 0:QL], v_[:, 0:QL], lri[:, t, 0:1], lat_w[:, 0:QL], ALU.mult, ALU.mult))
                    stt(lat[:, t, QL:QL + KVL], v_[:, QL:QL + KVL], lri[:, t, 1:2], lat_w[:, QL:QL + KVL],
                        ALU.mult, ALU.mult).then_inc(s["lat_h"], 1)
                if l == 0:
                    dve.wait_ge(s_small[2], 16)
                    dve.wait_ge(s_small[3], 16)
                dve.wait_ge(s["g1_used"], 4 * (l + 1))
                dtb = adt[:, l, 1:2, :].to_broadcast([P, TT, H])
                link(tt(sp[:, 0, :, :], abr[:, :, 0:H], dtb, ALU.add))
                link(ts(sp[:, 5, :, :], sp[:, 0, :, :], -1.0, None, ALU.mult))
                tt(sp[:, 1, :, :], sp[:, 0, :, :], sp[:, 5, :, :], ALU.min).then_inc(s["g_ready"], 1)
                upto(base, first["wkv"])
                for t in range(TT):
                    dve.wait_ge(s["lat_hi"], TT * l + t + 1)
                    sl = slice(t * P, (t + 1) * P)
                    tt(pT_lo[:, :, sl], two(6 - 6 * t)[:, 0:LC * P].rearrange("p (k n) -> p k n", k=LC),
                       pT_hi[:, :, sl].bitcast(F32), ALU.subtract).then_inc(s["lat_lo"], 1)
                upto(base, first["wq"] + 2)

                def rope(dst1, dst2, t1, t2, cos, sin, u):
                    link(tt(tmp_r[:, 0, 0:u, :], t1, sin, ALU.mult))
                    link(tt(tmp_r[:, 1, 0:u, :], t2, sin, ALU.mult))
                    link(tt(dst1, t1, cos, ALU.mult))
                    link(tt(dst2, t2, cos, ALU.mult))
                    link(tt(dst1, dst1, tmp_r[:, 1, 0:u, :], ALU.subtract))
                    return tt(dst2, dst2, tmp_r[:, 0, 0:u, :], ALU.add)

                if l == 0:
                    dve.wait_ge(s["trig"], 3)
                for t in range(TT):
                    c, sn = (b[:, t:t + 1, :] for b in (cosb, sinb))
                    t1, t2 = krr[:, t:t + 1, 0:HALF], krr[:, t:t + 1, HALF:ROPE]
                    link(rope(t1, t2, t1, t2, c, sn, 1))
                    v.tensor_copy(km[:, t, :, NOPE:DQ], krr[:, t:t + 1, :].to_broadcast([P, HM, ROPE])
                                  ).then_inc(s["k_rope"], 1)
                upto(base, first["qkv"] + 2)
                dve.wait_ge(s["q_copied"], TT * (l + 1))
                for t in range(TT):
                    c, sn = (b[:, t:t + 1, :].to_broadcast([P, HM, HALF]) for b in (cosb, sinb))
                    t1, t2 = qm[:, t, :, NOPE:NOPE + HALF], qm[:, t, :, NOPE + HALF:DQ]
                    rope(t1, t2, t1, t2, c, sn, HM).then_inc(s["q_rope"], 1)
                    dve.wait_ge(s["q_rope"], TT * l + t + 1)

                def scores(u):
                    nh, nk = (HM, P) if u == 0 else (HM // 2, T)
                    dve.wait_ge(s["sc_done"], 3 * l + u + 1)
                    sc = two(3).rearrange("p (h n) -> p h n", n=nk)
                    link(v.memset(sc[0:CHUNK, :, nk - CHUNK:nk], -BIG))
                    link(v.tensor_reduce(mx[:, u, 0:nh], sc, AX_X, ALU.max))
                    ts(mx[:, u, 0:nh], mx[:, u, 0:nh], -(float(DQ) ** -0.5), None, ALU.mult
                       ).then_inc(s["sc_masked"], 1)

                def outs(u):
                    h0, nh, t = (0, HM, 0) if u == 0 else ((u - 1) * HM // 2, HM // 2, 1)
                    dve.wait_ge(s["pv_done"], 3 * l + u + 1)
                    link(v.reciprocal(ri[:, u, 0:nh], rs[:, u, 0:nh]))
                    i = tt(om[:, t, h0 * VD:(h0 + nh) * VD].rearrange("p (h d) -> p h d", h=nh),
                           ps[:, 7, h0 * VD:(h0 + nh) * VD].rearrange("p (h d) -> p h d", h=nh),
                           bc(ri[:, u, 0:nh], VD), ALU.mult)
                    i.then_inc(s["o_norm"], 1) if u != 1 else link(i)
                    if u == 1:
                        return

                upto(base, first["qkv"] + 10)
                scores(0)
                upto(base, first["qkv"] + 12)
                scores(1)
                upto(base, first["qkv"] + 14)
                outs(0)
                scores(2)
                upto(base, first["qkv"] + 16)
                outs(1)
                v.memset(tick[:, :], 0.0).then_inc(s["x_ready"], 1)
                outs(2)
                upto(base, first["gate"] + 3)
                for t in range(TT):
                    dve.wait_ge(s["om_hi"], TT * l + t + 1)
                    sl = slice(t * P, (t + 1) * P)
                    tt(oT_lo[:, :, sl], ps[:, 4 + t, :].rearrange("p (k n) -> p k n", n=P),
                       oT_hi[:, :, sl].bitcast(F32), ALU.subtract).then_inc(s["om_lo"], 1)
                v.memset(pad[:, :, 0:3], 0.0).then_inc(s["pad_ready"], 1)
                if l == 0:
                    dve.wait_ge(s["cw_ready"], L)
                prev = [None] * NQK
                for k in range(1, CONV):
                    for c in range(NQK):
                        if k == 1:
                            dve.wait_ge(s["tap0"], NQK * l + c + 1)
                        else:
                            ch.wait(prev[c])
                        prev[c] = mark(stt(qkv[:, c, :], pad[:, c, k:k + T], cw[:, l, k, c:c + 1], qkv[:, c, :],
                                           ALU.mult, ALU.add))
                ch.wait(ch.n)
                v.memset(tick[:, :], 0.0).then_inc(s["conv_done"], 1)
                dve.wait_ge(s["g_ready"], 3 * l + 2)
                link(ts(sp[:, 0, :, :], sp[:, 0, :, :], 0.0, None, ALU.max))
                link(tt(sp[:, 0, :, :], sp[:, 0, :, :], sp[:, 3, :, :], ALU.add))
                link(ts(sp[:, 4, :, :], sp[:, 4, :, :], 1.0, None, ALU.add))
                link(v.reciprocal(beta[:, :, :], sp[:, 4, :, :]))
                stt(gl[:, :, :], sp[:, 0, :, :], -1.0, adt[:, l, 0:1, :].to_broadcast([P, TT, H]),
                    ALU.mult, ALU.mult).then_inc(s["g_ready"], 1)
                upto(base, first["gate"] + 8)
                dve.wait_ge(s["sums_done"], l + 1)
                v.tensor_copy(sums[:, 0:48], ps[:, 7, 0:48]).then_inc(s["sums_used"], 1)
                dve.wait_ge(s["sums_used"], l + 1)
                dve.wait_ge(s["lnrow"], l + 1)
                G, GL = (sums[:, j:j + 8].rearrange("p (t h) -> p t h", t=TT) for j in (16, 24))
                link(ts(gcol[:, 2, :, :], gcol[:, 0, :, :], -0.5, float(np.log(float(DV) ** -0.5)), ALU.mult, ALU.add))
                link(ts(gcol[:, 3, :, :], gcol[:, 1, :, :], 0.5, None, ALU.mult))
                link(tt(gcol[:, 4, :, :], G, gcol[:, 3, :, :], ALU.subtract))
                link(tt(gcol[:, 5, :, :], G, gcol[:, 3, :, :], ALU.add))
                link(ts(gcol[:, 5, :, :], gcol[:, 5, :, :], -1.0, None, ALU.mult))
                tt(gcol[:, 6, :, :], GL, gcol[:, 5, :, :], ALU.add).then_inc(s["lncols"], 1)
                dve.wait_ge(s["cols_ready"], l + 1)
                link(tt(gcol[:, 9, :, :], gcol[:, 7, :, :], beta[:, :, :], ALU.mult))
                upto(base, first["gate"] + 9)
                def gate_bias(hf):
                    r = 4 * l + 1 + hf
                    dve.wait_ge(w_used, base + first["gate"] + KC * (hf + 1))
                    dve.wait_ge(s_row[r % 2], 16 * (r // 2 + 1))
                    for t in range(TT):
                        tt(gates[:, t, hf * D:(hf + 1) * D], two(2 * t), rows[:, r % 2, :], ALU.add
                           ).then_inc(s["gate_in"], 1)
                    dve.wait_ge(s["gate_in"], 4 * l + 2 * (hf + 1))
                    v.memset(tick[:, :], 0.0).then_inc(row_used, 1)

                if l == 0:
                    dve.wait_ge(s["consts"], 1)
                for t in range(TT):
                    dve.wait_ge(s["row_exp"], TT * l + t + 1)
                    link(tt(inT[:, t, :].rearrange("p (h n) -> p h n", h=H),
                            ps[:, 4 + t, :].rearrange("p (h n) -> p h n", h=H),
                            neg_q[:, :].unsqueeze(1).to_broadcast([P, H, P]), ALU.add))
                    tt(Lm[:, t, :].rearrange("p (h n) -> p h n", h=H),
                       ps[:, 6 + t, :].rearrange("p (h n) -> p h n", h=H),
                       neg_k[:, :].unsqueeze(1).to_broadcast([P, H, P]), ALU.add).then_inc(s["eq_in"], 1)
                for t in range(TT):
                    sl = slice(t * P, (t + 1) * P)
                    link(tt(qdT[:, :, sl], qdT[:, :, sl], qkv[:, 0:H, sl], ALU.mult))
                for t in range(TT):
                    dve.wait_ge(s["kk_done"], TT * l + t + 1)
                    dve.wait_ge(s["e_exp"], 16 * l + 8 * (t + 1))
                    for h in range(H):
                        hs = slice(h * P, (h + 1) * P)
                        mark(stt(Lm[:, t, hs], Lm[:, t, hs], beta[:, t, h:h + 1], ps[:, 4 + t, hs],
                                 ALU.mult, ALU.mult))
                    mark(tt(inT[:, t, :], inT[:, t, :], ps[:, 6 + t, :], ALU.mult))
                    ch.wait(ch.n)
                    v.memset(tick[:, :], 0.0).then_inc(s["L_ready"], 1)
                upto(base, first["gate"] + 10)
                gate_bias(0)
                for t in range(TT):
                    dve.wait_ge(s["kt_done"], 2 * TT * l + t + 1)
                    kp = ps[:, 6 + t, :].rearrange("p (h n) -> p h n", h=H)
                    mark(tt(kb[:, t, :].rearrange("p (h n) -> p h n", h=H), kp, bc(gcol[:, 9, t, :], P), ALU.mult))
                    tt(kd[:, t, :].rearrange("p (h n) -> p h n", h=H), kp, bc(gcol[:, 8, t, :], P),
                       ALU.mult).then_inc(s["kt_used"], 1)
                m3 = lambda m: m.unsqueeze(1).to_broadcast([P, H, P])
                r3 = lambda b, t: b[:, t, :].rearrange("p (h n) -> p h n", h=H)
                for t in range(TT):
                    dve.wait_ge(s["LT_ready"], TT * l + t + 1)
                    link(tt(r3(X, t), r3(Lm, t), m3(lev0[:, :]), ALU.mult))
                    link(tt(r3(X, t), m3(ident[:, :]), r3(X, t), ALU.subtract))
                    link(tt(r3(XT, t), r3(LT, t), m3(lev[:, 0, :]), ALU.mult))
                    link(tt(r3(XT, t), m3(ident[:, :]), r3(XT, t), ALU.subtract))
                    tt(r3(MT, t), r3(LT, t), m3(lev[:, 1, :]), ALU.mult).then_inc(s["inv_ready"], 1)
                for t in range(TT):
                    dve.wait_ge(s["kt_done"], 2 * TT * l + TT + t + 1)
                    tt(r3(vb, t), ps[:, 6 + t, :].rearrange("p (h n) -> p h n", h=H), bc(beta[:, t, :], P),
                       ALU.mult).then_inc(s["kt_used"], 1)

                for k in range(1, NLEV):
                    upto(base, first["gate"] + min(11 + k, 16))
                    if k < NLEV - 1:
                        for t in range(TT):
                            dve.wait_ge(s["y_done"], (5 * l + k - 1) * TT + t + 1)
                            mark(tt(r3(MT, t), r3(LT, t), m3(lev[:, k + 1, :]), ALU.mult))
                    for t in range(TT):
                        dve.wait_ge(s["zz_done"], (5 * l + k - 1) * TT + t + 1)
                        if k < NLEV - 1:
                            mark(tt(r3(X, t), r3(X, t), ps[:, 6, :].rearrange("p (h n) -> p h n", h=H), ALU.subtract))
                        mark(tt(r3(XT, t), r3(XT, t), ps[:, 7, :].rearrange("p (h n) -> p h n", h=H), ALU.subtract))
                        ch.wait(ch.n)
                        v.memset(tick[:, :], 0.0).then_inc(s["inv_ready"], 1)
                upto(base, first["mla_o"] + 2)
                gate_bias(1)
                dve.wait_ge(s["w_done"], TT * (l + 1))
                for t in range(TT):
                    link(v.tensor_copy(ub[:, t, :], ps[:, 6 + t, :]))
                v.memset(tick[:, :], 0.0).then_inc(s["u_ready"], 1)
                for c in range(4):
                    t, r = c // 2, slice((c % 2) * CHUNK, (c % 2 + 1) * CHUNK)
                    if c:
                        dve.wait_ge(s["v_done"], 3 * l + c)
                        tt(vnb[r, t, :], ub[r, t, :], ps[r, 4, :], ALU.subtract).then_inc(s["vn_ready"], 1)
                        if c < 3:
                            link(tt(r3(S, c % 2), r3(S, 1 - c % 2), bc(cdb[:, c, :], P), ALU.mult))
                    else:
                        v.tensor_copy(vnb[r, t, :], ub[r, t, :]).then_inc(s["vn_ready"], 1)
                    if c < 3:
                        dve.wait_ge(s["s_done"], 3 * l + c + 1)
                        if c == 0:
                            v.tensor_copy(S[:, 0, :], ps[:, 5, :]).then_inc(s["s_ready"], 1)
                        else:
                            tt(S[:, c % 2, :], S[:, c % 2, :], ps[:, 5, :], ALU.add).then_inc(s["s_ready"], 1)
                        dve.wait_ge(s["s_ready"], 3 * l + c + 1)
                og = X
                upto(base, first["mla_o"] + 4)
                dve.wait_ge(s_small[6], 16 * (l + 1))
                dve.wait_ge(s["z_ready"], TT * (l + 1))
                for t in range(TT):
                    link(tt(r3(zs, t), r3(zs, t), onorm[:, :].unsqueeze(1).to_broadcast([P, H, P]), ALU.mult))
                for t in range(TT):
                    dve.wait_ge(s["o_ss"], H * (TT * l + t + 1))
                    link(tt(og[:, t, :], zs[:, t, :], ps[:, 6 + t, :], ALU.mult))
                    dve.wait_ge(s["o_r"], TT * l + t + 1)
                    tt(r3(og, t), r3(og, t), bc(ori[:, t, :], P), ALU.mult).then_inc(s["og_ready"], 1)
                upto(base, first["gdn_o"] + 2)
                for t in range(TT):
                    dve.wait_ge(s["og_hi"], TT * l + t + 1)
                    sl = slice(t * P, (t + 1) * P)
                    tt(pT_lo[:, 0:H, sl], ps[:, 4 + t, :].rearrange("p (k n) -> p k n", n=P),
                       pT_hi[:, 0:H, sl].bitcast(F32), ALU.subtract).then_inc(s["og_lo"], 1)
                dve.wait_ge(s["gate_ready"], 4 * (l + 1))
                dve.wait_ge(w_used, base + first["gdn_o"])
                for t in range(TT):
                    upto(base, first["gdn_o"] + 3 + t)
                    tt(gates[:, t, D:2 * D], gates[:, t, D:2 * D], two(2 * t), ALU.mult).then_inc(s["oa_in"], 1)
                upto(base, first["out"])
                dve.wait_ge(s["oa_in"], TT * (l + 1))
                for t in range(TT):
                    if t == 0:
                        dve.wait_ge(s["gdn_half"], l + 1)
                    else:
                        dve.wait_ge(w_used, base + first["out"])
                    link(tt(gates[:, t, 0:D], gates[:, t, 0:D], two(4 + 2 * t), ALU.mult))
                    tt(hbuf[:, t, :], gates[:, t, 0:D], gates[:, t, D:2 * D], ALU.add).then_inc(s["merged"], 1)
                upto(base, first["out"] + 3)
                for t in range(TT):
                    dve.wait_ge(s["m_hi"], TT * l + t + 1)
                    sl = slice(t * P, (t + 1) * P)
                    tt(aT_lo[:, :, sl], two(2 * t).rearrange("p (k n) -> p k n", k=KC),
                       aT_hi[:, :, sl].bitcast(F32), ALU.subtract).then_inc(s["m_lo"], 1)
                upto(base, N_MIX)
                for t in range(TT):
                    if t == 0:
                        dve.wait_ge(s["out_half"], l + 1)
                    else:
                        dve.wait_ge(w_used, base + N_MIX)
                    tt(x[:, t, :], x[:, t, :], two(4 + 2 * t), ALU.add).then_inc(s["x_new"], 1)

                if l == 0:
                    norm(1, 3, lambda k: split(At(DENSE + k), 2 * SUB))

                    def transposed(i, d, k0):
                        for t in range(TT):
                            dve.wait_ge(s["hT_hi"], At(t + 1 - d * TT, i, TT).count())
                            tt(dT_lo[:, bass.ds(k0, 7), t * P:(t + 1) * P],
                               two(4 + 2 * t)[:, 0:2 * SUB].rearrange("p (k n) -> p k n", n=P),
                               dT_hi[:, bass.ds(k0, 7), t * P:(t + 1) * P].bitcast(F32),
                               ALU.subtract).then_inc(s["hT_lo"], 1)

                    def up(i):
                        for j in range(0 if i is not None else TT + 1, N_UP):
                            split(At(DENSE + j, i, N_UP), 2 * SUB)
                            if j == 3 + SPL and i is not None:
                                transposed(i, 1, i * 7 - 7)
                            if j in (10, 15):
                                sub = j // 12
                                dve.wait_ge(w_used, At(DENSE + 8 * sub + 8, i, N_UP).count())
                                dve.wait_ge(s["h1_used"], At(sub + 1, i, 2).count())
                                tt(dhid[:, :, sub * SUB:(sub + 1) * SUB], dsil[:, sub, :, :], ps[:, 2:4, 0:SUB],
                                   ALU.mult).then_inc(s["h3_used"], 1)

                    up(None)
                    with dve.Fori(1, UPS) as i:
                        up(i)
                    split(At(MIX1 - N_DOWN), D)
                    transposed(None, 1 - UPS, N_DOWN - 7)
                    for k in range(1, N_DOWN):
                        split(At(DENSE + UPS * N_UP + k), D)
                    for t in range(TT):
                        if t == 0:
                            dve.wait_ge(s["down_half"], 1)
                        else:
                            dve.wait_ge(w_used, MIX1)
                        tt(x[:, t, :], x[:, t, :], two(2 * t), ALU.add).then_inc(s["x_new"], 1)
                else:
                    norm(3, 7, None, False)
                    for t in range(TT):
                        link(v.tensor_copy(y_hi[:, 0:2].bitcast(F32), hbuf[:, t, 0:2])) if False else None
                        v.memset(cmax[:, 0:1], 0.0).then_inc(s["sel_in"], 1)
                        dve.wait_ge(s["sel_in"], t + 1)
                    dve.wait_ge(s["lg_done"], 1)
                    link(v.tensor_copy(lg[:, :, :], ps[:, 0, 0:TT * NE].rearrange("p (t e) -> p t e", t=TT)))
                    for t in range(TT):
                        link(v.max(top[:, t, :], lg[:, t, :]))
                        link(v.max_index(topi[:, t, :], top[:, t, :], lg[:, t, :]))
                    link(v.tensor_copy(topf[:, :, :], topi[:, :, 0:TOP_K]))
                    for k in range(TOP_K):
                        for t in range(TT):
                            link(ts(oneh[:, k, t, :], slot_no[:, 0, 0:NE], -1.0, topf[:, t, k:k + 1],
                                    ALU.add, ALU.is_equal))
                    link(tt(mask[:, :, :], oneh[:, 0, :, :], oneh[:, 1, :, :], ALU.add))
                    tt(tw[:, :, 0:1], top[:, :, 1:2], top[:, :, 0:1], ALU.subtract).then_inc(s["lg_ready"], 1)
                    for t in range(TT):
                        dve.wait_ge(s["e_ready"], t + 1)
                        mark(tt(h2_lo[:, t, :], hbuf[:, t, :], h2_hi[:, t, :].bitcast(F32), ALU.subtract))
                    dve.wait_ge(s["e_ready"], TT + 1)
                    link(ts(tw[:, :, 2:3], tw[:, :, 1:2], 1.0, None, ALU.add))
                    link(v.reciprocal(tw[:, :, 2:3], tw[:, :, 2:3]))
                    link(tt(tw[:, :, 3:4], tw[:, :, 1:2], tw[:, :, 2:3], ALU.mult))
                    for t in range(TT):
                        w = comb[:, t, 1:NE + 1]
                        link(v.memset(comb[:, t, 0:1], 0.0))
                        link(v.memset(rank[:, t, NE:NE + 1], 0.0))
                        link(ts(w, oneh[:, 0, t, :], tw[:, t, 2:3], None, ALU.mult))
                        link(stt(w, oneh[:, 1, t, :], tw[:, t, 3:4], w, ALU.mult, ALU.add))
                    link(v.memset(y_hi[:, :].bitcast(F32), 0.0))
                    link(v.memset(y_lo[:, :].bitcast(F32), 0.0))
                    link(v.memset(selT[:, :].bitcast(F32), 0.0))
                    dve.wait_ge(s["rank_done"], 1)
                    pr = ps[:, 1, 0:3 * NE].rearrange("p (t e) -> p t e", t=3)
                    rk = rank[:, :, 0:NE]
                    link(ts(rk, pr[:, 0:2, :], 1.0, None, ALU.add))
                    link(v.tensor_reduce(cmax[:, 0:1], pr[:, 2, :], AX_X, ALU.max))
                    link(tt(rk, rk, mask[:, :, :], ALU.mult))
                    v.memset(cmax[:, 1:2], 0.0).then_inc(s["rank_ready"], 1)
                    ts(flag[:, :], cmax[:, 0:1], float(P), None, ALU.is_gt).then_inc(s["rank_ready"], 1)
                    dve.wait_ge(s["rank_ready"], 2)

                    def select(e, c, r, per):
                        for t in range(TT):
                            i = ts(sel[:, t, :], slot_no[:, r, :], rank[:, t, c], None, ALU.is_equal)
                            i.then_inc(s["sel_ready"], 1)

                    def back(e, c, t, col):
                        dve.wait_ge(s["sct_done"], c)
                        stt(x[:, t, :], two(6), comb[:, t, col], x[:, t, :], ALU.mult, ALU.add
                            ).then_inc(s["sct_used"], 1)

                    def experts(base, r):
                        select(None, slice(0, 1), r, 0)
                        with dve.Fori(0, NE) as e:
                            def halves(c):
                                return At(8 + 16 * r + c, e, 2).count()

                            for j in range(N_EXP):
                                split(At(base + j, e, N_EXP), EXP_COLS[j])
                                if j in (7, 11):
                                    t = j // 8
                                    if t == 0:
                                        dve.wait_ge(s["x_new"], 3 * TT)
                                    back(e, At(18 * r + t + 1, e, 2).count(), t, bass.ds(e, 1))
                                if j == 16:
                                    dve.wait_ge(s["selT_done"], At(8 * r + 1, e, 1).count())
                                    select(e, bass.ds(e + 1, 1), r, 2)
                                if j in (19, 35):
                                    hf = j // 32
                                    dve.wait_ge(w_used, At(base + (2 * hf + 2) * KC, e, N_EXP).count())
                                    dve.wait_ge(s["h1_used"], halves(hf + 1))
                                    tt(ehid[:, hf * HC:(hf + 1) * HC].rearrange("p (a n) -> p a n", a=2),
                                       esil[:, :].rearrange("p (a n) -> p a n", a=2), ps[:, 2:4, 0:HC // 2],
                                       ALU.mult).then_inc(s["h3_used"], 1)
                                if j in (23, 38):
                                    hf = j // 32
                                    dve.wait_ge(s["hT_hi"], halves(hf + 1))
                                    cs = slice(hf * EC // 2, (hf + 1) * EC // 2)
                                    tt(eT_lo[:, cs, :], two(6)[:, 0:HC].rearrange("p (k n) -> p k n", n=P),
                                       eT_hi[:, cs, :].bitcast(F32), ALU.subtract).then_inc(s["hT_lo"], 1)
                            dve.wait_ge(s["ey_hi"], At(8 * r + 1, e, 1).count())
                            tt(y_lo[:, :], two(4), y_hi[:, :].bitcast(F32), ALU.subtract).then_inc(s["ey_lo"], 1)
                        for t in range(TT):
                            back(None, 18 * r + 2 * NE + t + 1, t, slice(NE, NE + 1))
                        dve.wait_ge(s["sct_used"], 18 * (r + 1))

                    ch.wait(ch.n)
                    experts(MOE, 0)
                    over = dve.value_load(flag[0:1, 0:1], min_val=0, max_val=1)
                    with dve.If(over):
                        experts(OVER, 1)
                    v.memset(cmax[:, 1:2], 0.0).then_inc(s["over_done"], 1)
                    norm(2 * L, 8)

        @block.tensor
        def _(pe):
            mm = nc.tensor.matmul

            def prod(o, hi, lo, rhi, rlo, start, stop, skip=False):
                mm(o, hi, rhi, start=start, stop=False, skip_group_check=skip)
                mm(o, hi, rlo, start=False, stop=False, skip_group_check=skip)
                return mm(o, lo, rhi, start=False, stop=stop, skip_group_check=skip)

            def tile(t, n, c0=0):
                pe.wait_ge(w_lo, t.count(1))
                sl = t.c % SPL
                return whi[:, sl, c0:c0 + n], wlo[:, sl, c0:c0 + n]

            def by_token(base, name, j0, n, lhs, cols, bank, K=None, lead=0, trail=0, ready=None, half=None):
                K = K or n
                js = list(range(j0, j0 + n))
                groups = [js[0:lead]] if lead else []
                groups += [[j] for j in js[lead:n - trail]]
                if trail and lead < n:
                    groups.append(js[n - trail:])
                for g, group in enumerate(groups):
                    rhs = {}
                    for t in range(TT):
                        if g == 0 and ready:
                            ready(t)
                        sl = slice(t * P, (t + 1) * P)
                        for j in group:
                            T_ = At(base + first[name] + j)
                            if t == 0:
                                rhs[j] = tile(T_, sum(cols))
                            whs, wls = rhs[j]
                            k, c = j % K, 0
                            for b, w in enumerate(cols):
                                last = prod(ps[:, bank + 2 * t + b, 0:w], lhs[0][:, k, sl], lhs[1][:, k, sl],
                                            whs[:, c:c + w], wls[:, c:c + w], k == 0, k == K - 1)
                                c += w
                            if t == TT - 1:
                                last.then_inc(w_used, 1)
                        if t == 0 and half and g == len(groups) - 1:
                            last.then_inc(half, 1)

            def transposes(o, src, n, w=P):
                for k in range(n):
                    last = nc.tensor.transpose(o[0:w, k * P:(k + 1) * P], src[:, k * w:(k + 1) * w], ident[:, :])
                return last

            def norm(n):
                for t in range(TT):
                    pe.wait_ge(s["norm_h"], TT * n + t + 1)
                    transposes(two(4 + 2 * t), hbuf[:, t, :], KC).then_inc(s["norm_T"], 1)

            pe.wait_ge(s["ident_ready"], 1)

            for l in range(L):
                base = (MIX0, MIX1)[l]
                aT, pT, oT = (aT_hi, aT_lo), (pT_hi, pT_lo), (oT_hi, oT_lo)
                norm(2 * l)
                if l:
                    pe.wait_ge(s["x_new"], 2 * TT * l)
                by_token(base, "g1", 0, KC, aT, [512, G1 - 512], 0, lead=3,
                         ready=lambda t: pe.wait_ge(s["norm_lo"], TT * 2 * l + t + 1))
                if l == 0:
                    pe.wait_ge(s_small[1], 16)
                    for i in range(L):
                        nc.tensor.transpose(ps[:, 6 + i, 0:CONV * NQK], cw_in[:, i, :],
                                            ident[0:CONV * NQK, 0:CONV * NQK]).then_inc(s["cwT"], 1)
                for j in range(KC):
                    if j == 5:
                        if l == 0:
                            pe.wait_ge(s["cw_ready"], L)
                        for t in range(TT):
                            pe.wait_ge(s["lat_h"], TT * l + t + 1)
                            if t:
                                pe.wait_ge(s["g1_used"], 4 * (l + 1))
                            transposes(two(6 - 6 * t), lat[:, t, :], LC).then_inc(s["lat_T"], 1)
                    whs, wls = tile(At(base + first["z"] + j), QW)
                    for t in range(TT):
                        sl = slice(t * P, (t + 1) * P)
                        last = prod(ps[:, 4 + t, :], aT_hi[:, j, sl], aT_lo[:, j, sl], whs, wls, j == 0, j == KC - 1)
                    last.then_inc(w_used, 1)
                pe.wait_ge(s["lat_lo"], TT * (l + 1))
                kv = (pT_hi[:, QC:LC, :], pT_lo[:, QC:LC, :])
                by_token(base, "wkv", 0, LC - QC, kv, [512, 512], 0)
                pe.wait_ge(s["z_ready"], TT * (l + 1))
                by_token(base, "wq", 0, QC, pT, [512, QN - 512], 4)
                pe.wait_ge(s["kv_copied"], 2 * TT * (l + 1))

                def qkv_tiles(j0, n):
                    for j in range(j0, j0 + n):
                        hf, k = j // KC, j % KC
                        if j == KC:
                            pe.wait_ge(s["pad_ready"], 3 * l + 1)
                        whs, wls = tile(At(base + first["qkv"] + j), 3 * QW // 2)
                        for c in range(NQK // 2):
                            cs = slice(c * P, (c + 1) * P)
                            o = ps[:, c // 2, (c % 2) * T:(c % 2 + 1) * T]
                            last = prod(o, whs[:, cs], wls[:, cs], aT_hi[:, k, :], aT_lo[:, k, :],
                                        k == 0 and c % 2 == 0, k == KC - 1, True)
                        last.then_inc(w_used, 1)

                def qk_T(u):
                    src = (qm, km)[u // 2]
                    if u < 2:
                        pe.wait_ge(s["q_rope"], TT * l + u % 2 + 1)
                    else:
                        pe.wait_ge(s["k_rope"], TT * l + u % 2 + 1)
                        pe.wait_ge(s["qk_Tc"], 4 * l + u - 1)
                    o = two(4 + 2 * (u % 2))
                    for h in range(HM):
                        last = nc.tensor.transpose(o[0:DQ, h * P:(h + 1) * P], src[:, u % 2, h, :], ident[:, :])
                    last.then_inc(s["qk_T"], 1)

                def scores(u):
                    nh, nk, t = (HM, P, 0) if u == 0 else (HM // 2, T, 1)
                    if u:
                        pe.wait_ge(s["sc_exp"], 16 * l + (0, 8, 12)[u])
                    for h in range(nh):
                        hh = h + (HM // 2 if u == 2 else 0)
                        last = mm(two(3)[:, h * nk:(h + 1) * nk], qT[:, hh, t * P:(t + 1) * P], kT[:, hh, 0:nk],
                                  start=True, stop=True)
                    last.then_inc(s["sc_done"], 1)

                def p_T(u):
                    pe.wait_ge(s["sc_exp"], 16 * l + (8, 12, 16)[u])
                    if u:
                        pe.wait_ge(s["p_Tc"], 3 * l + u)
                    transposes(two(5), prob[:, u % 2, :], KC).then_inc(s["p_T"], 1)

                def pv(u):
                    nh, nk, h0 = (HM, 1, 0) if u == 0 else (HM // 2, TT, (u - 1) * HM // 2)
                    pe.wait_ge(s["p_Tc"], 3 * l + u + 1)
                    if u == 1:
                        pe.wait_ge(s["o_norm"], 2 * l + 1)
                    if u == 2:
                        pe.wait_ge(s["x_ready"], (l + 1) * 1)
                    for h in range(nh):
                        for k in range(nk):
                            c = h * nk + k
                            last = mm(ps[:, 7, (h0 + h) * VD:(h0 + h + 1) * VD], probT[:, u % 2, c * P:(c + 1) * P],
                                      vm[:, k, (h0 + h) * VD:(h0 + h + 1) * VD], start=(k == 0), stop=(k == nk - 1))
                    last.then_inc(s["pv_done"], 1)

                qkv_tiles(0, 4)
                qk_T(0)
                qk_T(1)
                qkv_tiles(4, 2)
                qk_T(2)
                qk_T(3)
                qkv_tiles(6, 2)
                pe.wait_ge(s["qk_Tc"], 4 * (l + 1))
                scores(0)
                qkv_tiles(8, 2)
                p_T(0)
                scores(1)
                qkv_tiles(10, 2)
                pv(0)
                p_T(1)
                scores(2)
                qkv_tiles(12, 2)
                pv(1)
                p_T(2)
                qkv_tiles(14, 2)
                pv(2)

                def gate_tiles(j0, n):
                    for j in range(j0, j0 + n):
                        if j == 0:
                            pe.wait_ge(s["pad_ready"], 3 * l + 2)
                            pe.wait_ge(s["sc_exp"], 16 * (l + 1))
                        if j == KC:
                            pe.wait_ge(s["gate_in"], 4 * l + 2)
                        by_token(base, "gate", j, 1, aT, [512, 512], 0, K=KC)

                gate_tiles(0, 1)
                pe.wait_ge(s["o_norm"], 2 * (l + 1))
                for t in range(TT):
                    transposes(ps[:, 4 + t, :], om[:, t, :], MV // P).then_inc(s["om_T"], 1)
                gate_tiles(1, 4)
                if l == 0:
                    pe.wait_ge(s["consts"], 1)
                pe.wait_ge(s["g_ready"], 3 * (l + 1))
                pe.wait_ge(s["sq_ready"], 2 * (l + 1))
                pe.wait_ge(s["om_lo"], TT * (l + 1))
                sq = (X, XT)
                for j in range(2):
                    for t in range(TT):
                        for h in range(H):
                            c = j * 8 + t * 4 + h
                            src = sq[j][:, :, :].rearrange("p a b -> p (a b)")[:, h * T + t * P:h * T + (t + 1) * P]
                            mm(ps[:, 7, c:c + 1], src, ones[:, 0:1], start=True, stop=True)
                for t in range(TT):
                    mm(ps[:, 7, 16 + 4 * t:20 + 4 * t], incl[:, :], gl[:, t, :], start=True, stop=True)
                    mm(ps[:, 7, 24 + 4 * t:28 + 4 * t], same[:, :], gl[:, t, :], start=True, stop=True)
                for c in range(4):
                    last = mm(ps[:, 7, 32 + 4 * c:36 + 4 * c], inchunk[:, c % 2:c % 2 + 1].to_broadcast([P, P]),
                              gl[:, c // 2, :], start=True, stop=True)
                last.then_inc(s["sums_done"], 1)
                gate_tiles(5, 2)
                pe.wait_ge(s["lncols"], l + 1)
                for t in range(TT):
                    for j in range(2):
                        for h in range(H):
                            o = ps[:, 4 + 2 * j + t, h * P:(h + 1) * P]
                            mm(o, gl[:, t, h:h + 1].to_broadcast([P, P]), incl[:, :], start=True, stop=False)
                            last = mm(o, gcol[:, 2 + j, t, h:h + 1].to_broadcast([P, P]), ident[:, :],
                                      start=False, stop=True)
                    last.then_inc(s["row_done"], 1)
                for t in range(TT):
                    pe.wait_ge(s["eq_in"], TT * l + t + 1)
                    sl = slice(t * P, (t + 1) * P)
                    for h in range(H):
                        mm(ps[:, 4 + t, h * P:(h + 1) * P], qkv[:, H + h, sl], qkv[:, H + h, sl], start=True, stop=True)
                        last = mm(ps[:, 6 + t, h * P:(h + 1) * P], qkv[:, H + h, sl], qkv[:, h, sl],
                                  start=True, stop=True)
                    last.then_inc(s["kk_done"], 1)
                gate_tiles(7, 1)
                for t in range(TT):
                    pe.wait_ge(s["L_ready"], TT * l + t + 1)
                    transposes(ps[:, 4 + t, :], Lm[:, t, :], H).then_inc(s["LT_done"], 1)
                for t in range(TT):
                    for h in range(H):
                        last = nc.tensor.transpose(ps[:, 6 + t, h * P:(h + 1) * P], qkv[:, H + h, t * P:(t + 1) * P],
                                                   ident[:, :])
                    last.then_inc(s["kt_done"], 1)
                for t in range(TT):
                    pe.wait_ge(s["kt_used"], 2 * TT * l + t + 1)
                    for h in range(H):
                        last = nc.tensor.transpose(ps[:, 6 + t, h * P:(h + 1) * P], qkv[:, 2 * H + h, t * P:(t + 1) * P],
                                                   ident[:, :])
                    last.then_inc(s["kt_done"], 1)
                gate_tiles(8, 2)
                for k in range(1, NLEV):
                    for t in range(TT):
                        pe.wait_ge(s["inv_ready"], TT * l * 6 + (k - 1) * TT + t + 1)
                        if k == 1:
                            pe.wait_ge(s["LT_ready"], TT * l + t + 1)
                            pe.wait_ge(s["kt_used"], 2 * TT * (l + 1))
                        for h in range(H):
                            hs = slice(h * P, (h + 1) * P)
                            last = mm(ps[:, 4 + t, hs], MT[:, t, hs], X[:, t, hs], start=True, stop=True)
                        last.then_inc(s["y_done"], 1)
                    for t in range(TT):
                        if t:
                            gate_tiles(9 + k, 1)
                            pe.wait_ge(s["inv_ready"], TT * l * 6 + TT + (k - 1) * TT + t)
                        pe.wait_ge(s["y_ready"], (5 * l + k - 1) * TT + t + 1)
                        for h in range(H):
                            hs = slice(h * P, (h + 1) * P)
                            if k < NLEV - 1:
                                mm(ps[:, 6, hs], XT[:, t, hs], Lm[:, t, hs], start=True, stop=True)
                            last = mm(ps[:, 7, hs], Lm[:, t, hs], XT[:, t, hs], start=True, stop=True)
                        last.then_inc(s["zz_done"], 1)
                gate_tiles(15, 1)
                pe.wait_ge(s["inv_ready"], TT * (l + 1) * 6)
                for t in range(TT):
                    for h in range(H):
                        hs = slice(h * P, (h + 1) * P)
                        mm(ps[:, 4 + t, hs], kb[:, t, hs], XT[:, t, hs], start=True, stop=True)
                        last = mm(ps[:, 6 + t, hs], XT[:, t, hs], vb[:, t, hs], start=True, stop=True)
                    last.then_inc(s["w_done"], 1)
                for c in range(4):
                    t, r = c // 2, slice((c % 2) * CHUNK, (c % 2 + 1) * CHUNK)
                    tk = slice(c * CHUNK, (c + 1) * CHUNK)
                    if c == 0:
                        pe.wait_ge(s["w_ready"], TT * (l + 1))
                        pe.wait_ge(s["u_ready"], l + 1)
                    else:
                        pe.wait_ge(s["s_ready"], 3 * l + c)
                        for h in range(H):
                            hs = slice(h * P, (h + 1) * P)
                            last = mm(ps[r, 4, hs], wTb[:, h, tk], S[:, 1 - c % 2, hs], start=True, stop=True)
                        last.then_inc(s["v_done"], 1)
                    if c in (1, 2):
                        if c == 1:
                            pe.wait_ge(s["gate_in"], 4 * (l + 1))
                        by_token(base, "mla_o", c - 1, 1, oT, [512, 512], 0, K=MV // P)
                    pe.wait_ge(s["vn_ready"], 4 * l + c + 1)
                    if c < 3:
                        for h in range(H):
                            hs = slice(h * P, (h + 1) * P)
                            last = mm(ps[:, 5, hs], kd[r, t, hs], vnb[r, t, hs], start=True, stop=True)
                        last.then_inc(s["s_done"], 1)
                    for h in range(H):
                        hs = slice(h * P, (h + 1) * P)
                        if c:
                            mm(ps[r, 6 + t, hs], qdT[:, h, tk], S[:, 1 - c % 2, hs], start=True, stop=False)
                        last = mm(ps[r, 6 + t, hs], inT[r, t, h * P + r.start:h * P + r.stop], vnb[r, t, hs],
                                  start=(c == 0), stop=True)
                    last.then_inc(s["o_done"], 1)
                for t in range(TT):
                    by_token(base, "mla_o", 2 + t, 1, oT, [512, 512], 0, K=MV // P)
                    pe.wait_ge(s["og_ready"], TT * l + t + 1)
                    transposes(ps[:, 4 + t, :], X[:, t, :], H).then_inc(s["og_T"], 1)
                pe.wait_ge(s["og_lo"], TT * (l + 1))
                by_token(base, "gdn_o", 0, H, pT, [512, 512], 4, trail=3, half=s["gdn_half"])
                pe.wait_ge(s["oa_in"], TT * (l + 1))
                for t in range(TT):
                    pe.wait_ge(s["merged"], TT * l + t + 1)
                    transposes(two(2 * t), hbuf[:, t, :], KC).then_inc(s["m_T"], 1)
                by_token(base, "out", 0, KC, aT, [512, 512], 4, lead=3, trail=3, half=s["out_half"],
                         ready=lambda t: pe.wait_ge(s["m_lo"], TT * l + t + 1))

                if l == 0:
                    norm(1)
                    def hidden_T(i, d):
                        pe.wait_ge(s["h3_used"], At(2 - 2 * d, i, 2).count())
                        for t in range(TT):
                            if i is not None and d == 1:
                                pass
                            transposes(two(4 + 2 * t), dhid[:, t, :], 7).then_inc(s["hT_done"], 1)

                    def up(i):
                        for sub in range(2):
                            for wi in range(2):
                                if wi == 1 and sub == 0 and i is not None:
                                    hidden_T(i, 1)
                                if sub:
                                    pe.wait_ge(s[("h1_used", "h3_used")[wi]], At(sub, i, 2).count())
                                elif i is not None and wi == 0:
                                    pe.wait_ge(s["h1_used"], At(0, i, 2).count())
                                begin = i is None and sub == 0 and wi == 0
                                for group in [[0, 1, 2], [3]] if begin else [[0], [1], [2], [3]]:
                                    rhs = {}
                                    for t in range(TT):
                                        if begin and group[0] == 0:
                                            pe.wait_ge(s["norm_lo"], TT + t + 1)
                                        sl = slice(t * P, (t + 1) * P)
                                        for j in group:
                                            if t == 0:
                                                rhs[j] = tile(At(DENSE + sub * 8 + wi * 4 + j, i, N_UP), 2 * SUB)
                                            whs, wls = rhs[j]
                                            for a in range(2):
                                                k, cs = 2 * j + a, slice(a * SUB, (a + 1) * SUB)
                                                last = prod(ps[:, 2 * wi + t, 0:SUB], aT_hi[:, k, sl],
                                                            aT_lo[:, k, sl], whs[:, cs], wls[:, cs],
                                                            k == 0, k == KC - 1)
                                            if t == TT - 1:
                                                last.then_inc(w_used, 1)
                        if i is not None:
                            pe.wait_ge(s["hT_lo"], At(0, i, TT).count())

                    up(None)
                    with pe.Fori(1, UPS) as i:
                        up(i)
                    for group in [[k] for k in range(N_DOWN - 3)] + [[N_DOWN - 3, N_DOWN - 2, N_DOWN - 1]]:
                        if group[0] == 1:
                            hidden_T(None, 1 - UPS)
                        if group[0] == N_DOWN - 7:
                            pe.wait_ge(s["hT_lo"], TT * UPS)
                        rhs = {}
                        for t in range(TT):
                            sl = slice(t * P, (t + 1) * P)
                            for k in group:
                                if t == 0:
                                    rhs[k] = tile(At(DENSE + UPS * N_UP + k), D)
                                whs, wls = rhs[k]
                                for b in range(2):
                                    cs = slice(b * 512, (b + 1) * 512)
                                    last = prod(ps[:, 2 * t + b, :], dT_hi[:, k, sl], dT_lo[:, k, sl],
                                                whs[:, cs], wls[:, cs], k == 0, k == N_DOWN - 1)
                                if t == TT - 1:
                                    last.then_inc(w_used, 1)
                            if t == 0 and len(group) > 1:
                                last.then_inc(s["down_half"], 1)
                else:
                    norm(3)
                    pe.wait_ge(s["norm_hi"], TT * 4)
                    pe.wait_ge(s_small[7], 16)
                    for t in range(TT):
                        for k in range(KC):
                            last = mm(ps[:, 0, t * NE:(t + 1) * NE], h2T[:, k, t * P:(t + 1) * P], rw[:, k, :],
                                      start=(k == 0), stop=(k == KC - 1))
                    last.then_inc(s["lg_done"], 1)
                    pe.wait_ge(s["lg_ready"], 1)
                    mm(ps[:, 1, 0:NE], upper[:, :], mask[:, 0, :], start=True, stop=True)
                    mm(ps[:, 1, NE:2 * NE], upper[:, :], mask[:, 1, :], start=True, stop=False)
                    mm(ps[:, 1, NE:2 * NE], ones[:, :], mask[:, 0, :], start=False, stop=True)
                    for t in range(TT):
                        last = mm(ps[:, 1, 2 * NE:3 * NE], ones[:, :], mask[:, t, :], start=(t == 0), stop=(t == 1))
                    last.then_inc(s["rank_done"], 1)
                    pe.wait_ge(s["rank_ready"], 2)

                    def gather(c, e, k):
                        src = (h2_hi, h2_lo)[k]
                        for f in range(KC):
                            for t in range(TT):
                                last = mm(two(6)[:, f * P:(f + 1) * P], src[:, t, f * P:(f + 1) * P],
                                          sel[:, t, :], start=(t == 0), stop=(t == TT - 1))
                        last.then_inc(s["gat_done"], 1)

                    def scatter(t):
                        for b in range(2):
                            sl, cs = slice(t * P, (t + 1) * P), slice(b * 512, (b + 1) * 512)
                            mm(ps[:, 6 + b, :], selT[:, sl], y_hi[:, cs], start=True, stop=False)
                            last = mm(ps[:, 6 + b, :], selT[:, sl], y_lo[:, cs], start=False, stop=True)
                        last.then_inc(s["sct_done"], 1)

                    def experts(base, r):
                        pe.wait_ge(s["sel_ready"], 18 * r + 2)
                        gather(18 * r, None, 0)
                        pe.wait_ge(s["gat_hi"], 18 * r + 1)
                        gather(18 * r, None, 1)
                        with pe.Fori(0, NE) as e:
                            def halves(c):
                                return At(8 + 16 * r + c, e, 2).count()

                            def pairs(c):
                                return At(18 * r + c, e, 2).count()

                            pe.wait_ge(s["gat_hi"], pairs(2))
                            for j in range(4 * KC):
                                wi, hf, k = (j // KC) % 2, j // (2 * KC), j % KC
                                if j == 4:
                                    if True:
                                        pe.wait_ge(s["ey_lo"], At(8 * r, e, 1).count()) if r else None
                                    scatter(0)
                                if j == 8:
                                    pe.wait_ge(s["sct_used"], pairs(1))
                                    scatter(1)
                                if j == 12:
                                    pe.wait_ge(s["sct_used"], pairs(2))
                                    for t in range(TT):
                                        last = mm(ps[:, 6, t * P:(t + 1) * P], sel[:, t, :], ident_r[:, :],
                                                  start=True, stop=True)
                                    last.then_inc(s["selT_done"], 1)
                                if j == 16:
                                    pe.wait_ge(s["h1_used"], halves(1))
                                if j == 20:
                                    pe.wait_ge(s["selT_used"], At(8 * r + 1, e, 1).count())
                                    pe.wait_ge(s["h3_used"], halves(1))
                                    transposes(two(6), ehid[:, 0:HC], EC // 2).then_inc(s["hT_done"], 1)
                                whs, wls = tile(At(base + j, e, N_EXP), HC)
                                for b in range(2):
                                    cs = slice(b * HC // 2, (b + 1) * HC // 2)
                                    last = prod(ps[:, 2 * wi + b, 0:HC // 2], gT_hi[:, k, :], gT_lo[:, k, :],
                                                whs[:, cs], wls[:, cs], k == 0, k == KC - 1)
                                last.then_inc(w_used, 1)
                            pe.wait_ge(s["sel_ready"], pairs(4))
                            pe.wait_ge(s["hT_lo"], halves(1))
                            gather(0, e, 0)
                            j = 4 * KC
                            for k in range(EC):
                                if k == 3:
                                    pe.wait_ge(s["gat_hi"], pairs(3))
                                    pe.wait_ge(s["h3_used"], halves(2))
                                    transposes(two(6), ehid[:, HC:FE], EC // 2).then_inc(s["hT_done"], 1)
                                if k == EC // 2:
                                    pe.wait_ge(s["hT_lo"], halves(2))
                                if k == 10:
                                    gather(0, e, 1)
                                for b in range(2):
                                    halved = k >= EC - 2
                                    T_ = At(base + j, e, N_EXP)
                                    if b == 0 or halved:
                                        whs, wls = tile(T_, D if not halved else D // 2)
                                    cs = slice(0, 512) if halved else slice(b * 512, (b + 1) * 512)
                                    last = prod(ps[:, 4 + b, :], eT_hi[:, k, :], eT_lo[:, k, :],
                                                whs[:, cs], wls[:, cs], k == 0, k == EC - 1)
                                    if b == 1 or halved:
                                        last.then_inc(w_used, 1)
                                        j += 1
                            assert j == N_EXP
                            pe.wait_ge(s["ey_lo"], At(8 * r + 1, e, 1).count())
                        pe.wait_ge(s["gat_hi"], 18 * (r + 1))
                        scatter(0)
                        pe.wait_ge(s["sct_used"], 18 * r + 2 * NE + 1)
                        scatter(1)

                    experts(MOE, 0)
                    over = pe.value_load(flag[0:1, 0:1], min_val=0, max_val=1)
                    with pe.If(over):
                        experts(OVER, 1)


_INS = ["x", "positions", "mix_norm", "w_in", "gate_bias", "conv_w", "a_log", "dt_bias", "gdn_out_norm", "w_gdn_o",
        "q_a_norm", "w_q_b", "kv_a_norm", "w_kv_b", "w_mla_o", "w_out", "ffn_norm", "dense_w1", "dense_w3",
        "dense_w2", "router_w", "moe_w1", "moe_w3", "moe_w2", "final_norm"]


def kernel(**inputs):
    import numpy as _np
    import concourse.bacc as _bacc
    from concourse import mybir as _mybir
    from concourse.bass_utils import run_bass_kernel_spmd as _run

    nc = _bacc.Bacc("TRN2", target_bir_lowering=False, num_devices=1)
    arrays, args = {}, {}
    for name in _INS:
        a = _np.ascontiguousarray(inputs[name])
        arrays[f"in_{name}"] = a
        args[name] = nc.dram_tensor(f"in_{name}", a.shape, _mybir.dt.from_np(a.dtype), kind="ExternalInput").ap()
    shape = inputs["x"].shape
    out = nc.dram_tensor("out_0", shape, _mybir.dt.float32, kind="ExternalOutput").ap()
    program(nc, args, out)
    r = _run(nc, [arrays], core_ids=[0])
    return r.results[0]["out_0"]
```
